# Optimizing a Trainium2 kernel written in Bass

```python
import jax, jax.numpy as jnp
from jax import lax
import numpy as np
import jax
import jax.numpy as jnp

D_MODEL = 1024
BATCH = 1
SEQ = 256
DEPTH = 1

EPS = 1e-6
CONV_WIDTH = D_MODEL
CONV_K = 3
GDN_HEADS = 8
GDN_DK = 128
GDN_DV = 128
GDN_CONV_K = 4
GDN_CHUNK = 64
GDN_QK = GDN_HEADS * GDN_DK
GDN_VW = GDN_HEADS * GDN_DV
D_FF = 256 * ((8 * D_MODEL // 3 + 255) // 256)
FFN_CONV_K = 3
IN_SPLITS = (CONV_WIDTH, CONV_WIDTH, CONV_WIDTH, GDN_QK, GDN_QK, GDN_VW, GDN_VW, GDN_HEADS, GDN_HEADS, D_MODEL, D_MODEL)
IN_WIDTH = sum(IN_SPLITS)


def _split_points():
    pts, acc = [], 0
    for w in IN_SPLITS[:-1]:
        acc += w
        pts.append(acc)
    return pts

def rmsnorm(x, g):
    xf = x.astype(jnp.float32)
    y = xf * lax.rsqrt(jnp.mean(xf * xf, axis=-1, keepdims=True) + EPS)
    return (y * g.astype(jnp.float32)).astype(x.dtype)

def l2norm(x):
    return x * lax.rsqrt(jnp.sum(x * x, axis=-1, keepdims=True) + EPS)

def causal_dwconv(x, w):
    K = w.shape[0]
    S = x.shape[1]
    xp = jnp.pad(x, ((0, 0), (K - 1, 0), (0, 0)))
    return sum(xp[:, j:j + S] * w[j] for j in range(K))

def short_conv_branch(bg, cg, xv, conv_w):
    return bg * causal_dwconv(cg * xv, conv_w)

def gated_delta_rule_chunked(q, k, v, g, beta):
    Bsz, S, H, dk = q.shape
    dv = v.shape[-1]
    C = GDN_CHUNK
    N = S // C

    def chunks(t):
        return t.reshape(Bsz, N, C, H, *t.shape[3:]).swapaxes(2, 3)

    q, k, v, g, beta = (chunks(t) for t in (q, k, v, g, beta))
    G = jnp.cumsum(g, axis=-1)
    tril = jnp.tril(jnp.ones((C, C), dtype=bool))
    strict = jnp.tril(jnp.ones((C, C), dtype=bool), -1)
    decay = jnp.exp(jnp.where(tril, G[..., :, None] - G[..., None, :], -jnp.inf))
    k_beta = k * beta[..., None]
    v_beta = v * beta[..., None]
    L = jnp.where(strict, jnp.einsum('bnhid,bnhjd->bnhij', k_beta, k) * decay, 0.0)
    eye = jnp.eye(C, dtype=q.dtype)
    rhs = jnp.concatenate([v_beta, k_beta * jnp.exp(G)[..., None]], axis=-1)
    sol = lax.linalg.triangular_solve(eye + L, rhs, left_side=True, lower=True)
    u, w = sol[..., :dv], sol[..., dv:]
    A_qk = jnp.einsum('bnhid,bnhjd->bnhij', q, k) * decay
    q_dec = q * jnp.exp(G)[..., None]
    G_last = G[..., -1:]
    k_dec = k * jnp.exp(G_last - G)[..., None]

    def step(state, inp):
        q_c, k_c, u_c, w_c, A_c, gl = inp
        v_new = u_c - jnp.einsum('bhcd,bhde->bhce', w_c, state)
        o = jnp.einsum('bhcd,bhde->bhce', q_c, state) + jnp.einsum('bhij,bhje->bhie', A_c, v_new)
        state = state * jnp.exp(gl)[..., None] + jnp.einsum('bhcd,bhce->bhde', k_c, v_new)
        return state, o

    xs = tuple(jnp.moveaxis(t, 1, 0) for t in (q_dec, k_dec, u, w, A_qk, G_last))
    state0 = jnp.zeros((Bsz, H, dk, dv), dtype=q.dtype)
    _, o = lax.scan(step, state0, xs)
    return o.transpose(1, 0, 3, 2, 4).reshape(Bsz, S, H, dv)

def gdn_branch(q, k, v, z, a, b, conv_w, A_log, dt_bias, norm_g):
    Bsz, S, _ = q.shape
    dtype = q.dtype
    f32 = jnp.float32
    qkv = jax.nn.silu(causal_dwconv(jnp.concatenate([q, k, v], axis=-1), conv_w))
    q, k, v = jnp.split(qkv, [GDN_QK, 2 * GDN_QK], axis=-1)
    q = l2norm(q.reshape(Bsz, S, GDN_HEADS, GDN_DK).astype(f32)) * (GDN_DK ** -0.5)
    k = l2norm(k.reshape(Bsz, S, GDN_HEADS, GDN_DK).astype(f32))
    v = v.reshape(Bsz, S, GDN_HEADS, GDN_DV).astype(f32)
    beta = jax.nn.sigmoid(b.astype(f32))
    g = -jnp.exp(A_log.astype(f32)) * jax.nn.softplus(a.astype(f32) + dt_bias.astype(f32))
    o = gated_delta_rule_chunked(q, k, v, g, beta)
    o = o * lax.rsqrt(jnp.mean(o * o, axis=-1, keepdims=True) + EPS) * norm_g.astype(f32)
    o = o * jax.nn.silu(z.reshape(Bsz, S, GDN_HEADS, GDN_DV).astype(f32))
    return o.reshape(Bsz, S, GDN_VW).astype(dtype)

def conv_ffn(h, w_up, conv_w, w_down):
    up = causal_dwconv(h @ w_up, conv_w)
    gate, val = jnp.split(up, [D_FF], axis=-1)
    return (jax.nn.silu(gate) * val) @ w_down

def first_inputs(seed: int = 0) -> dict:
    key = jax.random.key(seed)
    ks = jax.random.split(key, 16)
    f32 = jnp.float32
    nrm = lambda k, shape, scale: jax.random.normal(k, shape, f32) * scale
    x = jax.random.normal(ks[0], (BATCH, SEQ, D_MODEL), f32)
    norm_mix_g = 1.0 + nrm(ks[1], (DEPTH, D_MODEL), 0.02)
    w_in = nrm(ks[2], (DEPTH, D_MODEL, IN_WIDTH), D_MODEL ** -0.5)
    conv_a_w = nrm(ks[3], (DEPTH, CONV_K, CONV_WIDTH), CONV_K ** -0.5)
    gdn_conv_w = nrm(ks[4], (DEPTH, GDN_CONV_K, 2 * GDN_QK + GDN_VW), GDN_CONV_K ** -0.5)
    gdn_A_log = jnp.log(jax.random.uniform(ks[5], (DEPTH, GDN_HEADS), f32, 1.0, 16.0))
    dt = jnp.exp(jax.random.uniform(ks[6], (DEPTH, GDN_HEADS), f32, np.log(1e-3), np.log(1e-1)))
    gdn_dt_bias = dt + jnp.log(-jnp.expm1(-dt))
    gdn_norm_g = 1.0 + nrm(ks[7], (DEPTH, GDN_DV), 0.02)
    w_a_out = nrm(ks[8], (DEPTH, CONV_WIDTH, D_MODEL), CONV_WIDTH ** -0.5)
    w_b_out = nrm(ks[9], (DEPTH, GDN_VW, D_MODEL), GDN_VW ** -0.5)
    w_o = nrm(ks[10], (DEPTH, D_MODEL, D_MODEL), D_MODEL ** -0.5)
    norm_ffn_g = 1.0 + nrm(ks[11], (DEPTH, D_MODEL), 0.02)
    w_up = nrm(ks[12], (DEPTH, D_MODEL, 2 * D_FF), D_MODEL ** -0.5)
    ffn_conv_w = nrm(ks[13], (DEPTH, FFN_CONV_K, 2 * D_FF), FFN_CONV_K ** -0.5)
    w_down = nrm(ks[14], (DEPTH, D_FF, D_MODEL), D_FF ** -0.5)
    norm_final_g = 1.0 + nrm(ks[15], (D_MODEL,), 0.02)
    return {"x": x, "norm_mix_g": norm_mix_g, "w_in": w_in, "conv_a_w": conv_a_w,
            "gdn_conv_w": gdn_conv_w, "gdn_A_log": gdn_A_log, "gdn_dt_bias": gdn_dt_bias,
            "gdn_norm_g": gdn_norm_g, "w_a_out": w_a_out, "w_b_out": w_b_out, "w_o": w_o,
            "norm_ffn_g": norm_ffn_g, "w_up": w_up, "ffn_conv_w": ffn_conv_w, "w_down": w_down,
            "norm_final_g": norm_final_g}

def first_block(x, norm_mix_g, w_in, conv_a_w, gdn_conv_w, gdn_A_log, gdn_dt_bias, gdn_norm_g,
              w_a_out, w_b_out, w_o, norm_ffn_g, w_up, ffn_conv_w, w_down, norm_final_g):
    pts = _split_points()
    for l in range(DEPTH):
        h = rmsnorm(x, norm_mix_g[l])
        proj = h @ w_in[l]
        bg, cg, xv, q, k, v, z, a, b, ga, gb = jnp.split(proj, pts, axis=-1)
        y_a = short_conv_branch(bg, cg, xv, conv_a_w[l]) @ w_a_out[l]
        y_b = gdn_branch(q, k, v, z, a, b, gdn_conv_w[l], gdn_A_log[l], gdn_dt_bias[l],
                         gdn_norm_g[l]) @ w_b_out[l]
        mix = jax.nn.sigmoid(ga) * y_a + jax.nn.sigmoid(gb) * y_b
        x = x + mix @ w_o[l]
        h = rmsnorm(x, norm_ffn_g[l])
        x = x + conv_ffn(h, w_up[l], ffn_conv_w[l], w_down[l])
    return rmsnorm(x, norm_final_g)


ATT_GROUPS = ((128, 1), (512, 4), (2048, 16))
ATT_HEADS_PER_GROUP = 4
ATT_HEADS = ATT_HEADS_PER_GROUP * len(ATT_GROUPS)
ATT_HEAD_DIM = 128
ATT_BLOCK = 128
ATT_W = ATT_HEADS * ATT_HEAD_DIM
ATT_OUT_W = ATT_HEADS_PER_GROUP * ATT_HEAD_DIM
RET_HEADS = 4
RET_QK_DIM = D_MODEL // RET_HEADS
RET_V_DIM = 2 * D_MODEL // RET_HEADS
RET_QK_W = RET_HEADS * RET_QK_DIM
RET_V_W = RET_HEADS * RET_V_DIM
RET_CHUNK = 128
D_FF_2 = 4 * D_MODEL
IN_SPLITS_2 = (ATT_W, ATT_W, ATT_W, RET_QK_W, RET_QK_W, RET_V_W, RET_V_W, D_MODEL, D_MODEL)
IN_W = sum(IN_SPLITS_2)


def rmsnorm_2(x, g):
    xf = x.astype(jnp.float32)
    y = xf * lax.rsqrt(jnp.mean(xf * xf, axis=-1, keepdims=True) + EPS)
    return (y * g.astype(jnp.float32)).astype(x.dtype)

def alibi_slopes(n_heads):
    return jnp.asarray(2.0 ** (-8.0 * np.arange(1, n_heads + 1, dtype=np.float32) / n_heads), dtype=jnp.float32)

def dilated_group(q, k, v, slopes, window, dilation):
    B, S, H, Dh = q.shape
    span = dilation * ATT_BLOCK
    s_pad = -(-S // span) * span
    L = s_pad // dilation
    nb = L // ATT_BLOCK
    reach = window // dilation

    def to_blocks(t):
        t = jnp.pad(t, ((0, 0), (0, s_pad - S), (0, 0), (0, 0)))
        t = t.reshape(B, L, dilation, H, Dh).transpose(0, 2, 3, 1, 4)
        return t.reshape(B, dilation, H, nb, ATT_BLOCK, Dh)

    def with_prev(t):
        prev = jnp.pad(t, ((0, 0), (0, 0), (0, 0), (1, 0), (0, 0), (0, 0)))[:, :, :, :-1]
        return jnp.concatenate([prev, t], axis=4)

    qb = to_blocks(q)
    kb = with_prev(to_blocks(k))
    vb = with_prev(to_blocks(v))
    s = jnp.einsum('brhnqd,brhnkd->brhnqk', qb, kb, preferred_element_type=jnp.float32) * (Dh ** -0.5)
    qi = jnp.arange(ATT_BLOCK)[:, None]
    kj = jnp.arange(2 * ATT_BLOCK)[None, :]
    dist = ATT_BLOCK + qi - kj
    blk = jnp.arange(nb)[:, None, None]
    valid = (dist >= 0) & (dist <= reach) & ((blk - 1) * ATT_BLOCK + kj >= 0)
    bias = -slopes[:, None, None] * (dist * dilation).astype(jnp.float32)
    s = jnp.where(valid[None, None, None], s + bias[None, None, :, None], -jnp.inf)
    m = jnp.max(s, axis=-1)
    p = jnp.exp(s - m[..., None])
    den = jnp.sum(p, axis=-1)
    o = jnp.einsum('brhnqk,brhnkd->brhnqd', p, vb.astype(jnp.float32)) / den[..., None]
    lse = m + jnp.log(den)
    o = o.reshape(B, dilation, H, L, Dh).transpose(0, 3, 1, 2, 4).reshape(B, s_pad, H, Dh)[:, :S]
    lse = lse.reshape(B, dilation, H, L).transpose(0, 3, 1, 2).reshape(B, s_pad, H)[:, :S]
    return o, lse

def retention(q, k, v):
    B, S, H, dk = q.shape
    dv = v.shape[-1]
    C = RET_CHUNK
    N = S // C
    log_g = jnp.log(1.0 - 2.0 ** (-5.0 - jnp.arange(H, dtype=jnp.float32)))
    idx = jnp.arange(C, dtype=jnp.float32)
    diff = idx[:, None] - idx[None, :]
    decay = jnp.where(diff >= 0, jnp.exp(log_g[:, None, None] * jnp.maximum(diff, 0.0)), 0.0)
    xi = jnp.exp(log_g[None, :] * (idx[:, None] + 1.0))
    zeta = jnp.exp(log_g[None, :] * (C - 1.0 - idx[:, None]))
    g_chunk = jnp.exp(log_g * C)
    qc = q.astype(jnp.float32).reshape(B, N, C, H, dk)
    kc = (k.astype(jnp.float32) * (dk ** -0.5)).reshape(B, N, C, H, dk)
    vc = v.astype(jnp.float32).reshape(B, N, C, H, dv)
    s = jnp.einsum('bnqhd,bnkhd->bnhqk', qc, kc) * decay[None, None]
    inner = jnp.einsum('bnhqk,bnkhv->bnqhv', s, vc)
    kz = kc * zeta[None, None, :, :, None]

    def step(state, xs):
        q_i, kz_i, v_i = xs
        cross = jnp.einsum('bqhd,bhdv->bqhv', q_i, state)
        state = state * g_chunk[None, :, None, None] + jnp.einsum('bkhd,bkhv->bhdv', kz_i, v_i)
        return state, cross

    state0 = jnp.zeros((B, H, dk, dv), jnp.float32)
    _, cross = lax.scan(step, state0, (qc.transpose(1, 0, 2, 3, 4), kz.transpose(1, 0, 2, 3, 4), vc.transpose(1, 0, 2, 3, 4)))
    cross = cross.transpose(1, 0, 2, 3, 4) * xi[None, None, :, :, None]
    return (inner + cross).reshape(B, S, H, dv)

def head_groupnorm(o, g, b):
    B, S, H, dv = o.shape
    mu = jnp.mean(o, axis=-1, keepdims=True)
    var = jnp.mean(jnp.square(o - mu), axis=-1, keepdims=True)
    y = ((o - mu) * lax.rsqrt(var + EPS)).reshape(B, S, H * dv)
    return y * g.astype(jnp.float32) + b.astype(jnp.float32)

def second_inputs(seed: int = 0) -> dict:
    key = jax.random.key(seed)
    ks = jax.random.split(key, 14)

    def nrm(k, shape, scale):
        return scale * jax.random.normal(k, shape, jnp.float32)

    return {
        'x': nrm(ks[0], (BATCH, SEQ, D_MODEL), 1.0),
        'norm1_g': 1.0 + nrm(ks[1], (DEPTH, D_MODEL), 0.02),
        'w_in': nrm(ks[2], (DEPTH, D_MODEL, IN_W), D_MODEL ** -0.5),
        'q_norm_g': 1.0 + nrm(ks[3], (DEPTH, ATT_HEADS, ATT_HEAD_DIM), 0.02),
        'k_norm_g': 1.0 + nrm(ks[4], (DEPTH, ATT_HEADS, ATT_HEAD_DIM), 0.02),
        'ret_gn_g': 1.0 + nrm(ks[5], (DEPTH, RET_V_W), 0.02),
        'ret_gn_b': nrm(ks[6], (DEPTH, RET_V_W), 0.02),
        'w_proj_a': nrm(ks[7], (DEPTH, ATT_OUT_W, D_MODEL), ATT_OUT_W ** -0.5),
        'w_proj_b': nrm(ks[8], (DEPTH, RET_V_W, D_MODEL), RET_V_W ** -0.5),
        'w_out': nrm(ks[9], (DEPTH, D_MODEL, D_MODEL), D_MODEL ** -0.5),
        'norm2_g': 1.0 + nrm(ks[10], (DEPTH, D_MODEL), 0.02),
        'w_up': nrm(ks[11], (DEPTH, D_MODEL, D_FF_2), D_MODEL ** -0.5),
        'w_down': nrm(ks[12], (DEPTH, D_FF_2, D_MODEL), D_FF_2 ** -0.5),
    }

def second_block(x, norm1_g, w_in, q_norm_g, k_norm_g, ret_gn_g, ret_gn_b, w_proj_a, w_proj_b, w_out, norm2_g, w_up, w_down):
    B, S, _ = x.shape
    slopes = alibi_slopes(ATT_HEADS)
    bounds = np.cumsum((0,) + IN_SPLITS_2).tolist()
    for l in range(DEPTH):
        xn = rmsnorm_2(x, norm1_g[l])
        wl = w_in[l]
        qa, ka, va, qr, kr, vr, gr, gate_a, gate_b = [xn @ wl[:, bounds[i]:bounds[i + 1]] for i in range(len(IN_SPLITS_2))]
        qa = rmsnorm_2(qa.reshape(B, S, ATT_HEADS, ATT_HEAD_DIM), q_norm_g[l])
        ka = rmsnorm_2(ka.reshape(B, S, ATT_HEADS, ATT_HEAD_DIM), k_norm_g[l])
        va = va.reshape(B, S, ATT_HEADS, ATT_HEAD_DIM)
        outs, lses = [], []
        for gi, (window, dilation) in enumerate(ATT_GROUPS):
            hs = slice(gi * ATT_HEADS_PER_GROUP, (gi + 1) * ATT_HEADS_PER_GROUP)
            o, lse = dilated_group(qa[:, :, hs], ka[:, :, hs], va[:, :, hs], slopes[hs], window, dilation)
            outs.append(o)
            lses.append(lse)
        alpha = jax.nn.softmax(jnp.stack(lses, axis=0), axis=0)
        o_a = jnp.sum(alpha[..., None] * jnp.stack(outs, axis=0), axis=0).reshape(B, S, ATT_OUT_W).astype(x.dtype)
        o_r = retention(qr.reshape(B, S, RET_HEADS, RET_QK_DIM), kr.reshape(B, S, RET_HEADS, RET_QK_DIM),
                        vr.reshape(B, S, RET_HEADS, RET_V_DIM))
        o_r = (head_groupnorm(o_r, ret_gn_g[l], ret_gn_b[l]) * jax.nn.silu(gr.astype(jnp.float32))).astype(x.dtype)
        y = jax.nn.sigmoid(gate_a) * (o_a @ w_proj_a[l]) + jax.nn.sigmoid(gate_b) * (o_r @ w_proj_b[l])
        x = x + y @ w_out[l]
        xn2 = rmsnorm_2(x, norm2_g[l])
        x = x + jnp.square(jax.nn.relu(xn2 @ w_up[l])) @ w_down[l]
    return x


def setup_inputs(seed=0):
    out = dict(first_inputs(seed))
    for name, value in second_inputs(seed + 1).items():
        if name != "x":
            out[name + "_2"] = value
    return out


def reference(
    x, norm_mix_g, w_in, conv_a_w, gdn_conv_w, gdn_A_log, gdn_dt_bias, gdn_norm_g, w_a_out,
    w_b_out, w_o, norm_ffn_g, w_up, ffn_conv_w, w_down, norm_final_g, norm1_g_2, w_in_2,
    q_norm_g_2, k_norm_g_2, ret_gn_g_2, ret_gn_b_2, w_proj_a_2, w_proj_b_2, w_out_2, norm2_g_2,
    w_up_2, w_down_2,
):
    x = first_block(
        x, norm_mix_g, w_in, conv_a_w, gdn_conv_w, gdn_A_log, gdn_dt_bias, gdn_norm_g, w_a_out,
        w_b_out, w_o, norm_ffn_g, w_up, ffn_conv_w, w_down, norm_final_g,
    )
    return second_block(
        x, norm1_g_2, w_in_2, q_norm_g_2, k_norm_g_2, ret_gn_g_2, ret_gn_b_2, w_proj_a_2,
        w_proj_b_2, w_out_2, norm2_g_2, w_up_2, w_down_2,
    )


_drawn_inputs = setup_inputs


def setup_inputs(seed=0):
    import zlib

    import numpy as np

    out = dict(_drawn_inputs(seed))
    spreads = {}
    factors = {'gdn_norm_g': 7.382,
     'norm_ffn_g': 3.359,
     'norm1_g_2': 3.732,
     'q_norm_g_2': 8.0,
     'k_norm_g_2': 8.0,
     'ret_gn_g_2': 21.916,
     'ret_gn_b_2': 21.526,
     'norm2_g_2': 11.662}
    for name, (base, spread) in spreads.items():
        noise = np.random.default_rng([zlib.crc32(name.encode()), seed]).standard_normal(out[name].shape)
        drawn = base * np.exp(spread * noise) if base else spread * noise
        out[name] = jnp.asarray(drawn.astype(out[name].dtype))
    for name, factor in factors.items():
        out[name] = (out[name] * factor).astype(out[name].dtype)
    return out
```

```python
from contextlib import ExitStack

import numpy as np

import concourse.bass as bass
from concourse import mybir

ALU = mybir.AluOpType
ACT = mybir.ActivationFunctionType
AX = mybir.AxisListType
F32 = mybir.dt.float32
F32R = mybir.dt.float32r

P = 128
D = 1024
S = 256
KT = D // P
EPS = 1e-6
H1 = 8
FF1 = 2816 // P
HA, HG = 12, 4
RH = 4
BIG = 1e30
NEG = -1e30
SCALE = float(P) ** -0.5


def plan():
    seq = [(kind, j) for kind in "kqv" for j in range(4)]
    seq += [(kind, j) for j in range(4) for kind in ("c", "x", "b")]
    seq += [(kind, j) for j in range(4) for kind in ("ga", "wa")]
    seq += [("gb", j) for j in range(4)] + [("z", j) for j in range(4)]
    seq += [("wb", j) for j in range(4)] + [("wo", j) for j in range(4)]
    seq += [("u1", j) for j in range(10)] + [("d1", j) for j in range(4)]
    seq += [("u1", j) for j in range(10, FF1)] + [("d1", j) for j in range(4, 11)]
    seq += [("qa", j) for j in range(6)] + [("ka", j) for j in range(6)] + [("va", j) for j in range(6)]
    seq += [("kr", j) for j in range(4)] + [("qr", j) for j in range(4)]
    seq += [("vr", j) for j in range(8)] + [("gr", j) for j in range(8)]
    seq += [("ta", j) for j in range(4)] + [("tb", j) for j in range(4)]
    seq += [("pa", j) for j in range(2)] + [("pb", j) for j in range(8)] + [("w2", j) for j in range(4)]
    seq += [("u2", j) for j in range(8)]
    for g in range(1, 4):
        seq += [("d2", 4 * (g - 1) + j) for j in range(4)]
        if g < 3:
            seq += [("u2", 4 * (g + 1) + j) for j in range(4)]
    seq += [("d2", 12 + j) for j in range(4)]
    return seq


SEQ = plan()
NB = len(SEQ)
AT = {key: n for n, key in enumerate(SEQ)}
COL1 = {"b": 0, "c": 8, "x": 16, "q": 24, "k": 32, "v": 40, "z": 48}
COL2 = {"qa": 0, "ka": 12, "va": 24, "qr": 36, "kr": 44, "vr": 52, "gr": 68, "ta": 84, "tb": 92}


def pairs(kind, j):
    two = [(k, c) for k in range(KT) for c in (2 * j, 2 * j + 1)]
    if kind in COL1:
        return "w_in", [(k, COL1[kind] + c) for k, c in two]
    if kind in ("ga", "gb"):
        return "w_gates", [(k, (0 if kind == "ga" else 8) + c) for k, c in two]
    if kind in ("wa", "wb", "wo", "w2"):
        return {"wa": "w_a_out", "wb": "w_b_out", "wo": "w_o", "w2": "w_out_2"}[kind], two
    if kind == "u1":
        return "w_up", [(k, c) for k in range(KT) for c in (j, FF1 + j)]
    if kind == "d1":
        every = [(k, c) for g in (0, 8) for q in range(4) for k in range(g, g + 8) for c in (2 * q, 2 * q + 1)]
        every += [(k, c) for c in range(KT) for k in range(16, FF1)]
        return "w_down", every[16 * j:16 * j + 16]
    if kind in COL2:
        return "w_in_2", [(k, COL2[kind] + c) for k, c in two]
    if kind == "pa":
        return "w_proj_a_2", [(k, c) for c in range(4 * j, 4 * j + 4) for k in range(4)]
    if kind == "pb":
        return "w_proj_b_2", [(8 * (j % 2) + k, 2 * (j // 2) + c) for k in range(8) for c in range(2)]
    if kind == "u2":
        return "w_up_2", two
    return "w_down_2", [(8 * (j // 4) + k, 2 * (j % 4) + c) for k in range(8) for c in range(2)]


PAR = {}
_at = 0
for _name, _n in (("g_mix", 8), ("conv_a", 24), ("conv_g", 96), ("g_ffn", 8), ("conv_f", 132), ("g_fin", 8),
                  ("g_n1", 8), ("g_q", 12), ("g_k", 12), ("gn_g", 16), ("gn_b", 16), ("g_n2", 8),
                  ("g_o", 1), ("a_log", 1), ("dt_b", 1), ("eps", 1), ("one", 1), ("ln_scale", 1),
                  ("ident", 128), ("ones", 128)):
    PAR[_name] = _at
    _at += _n
NPAR = _at
CHUNK = 64

RING = [key for key in SEQ if key[0] not in ("d1", "d2", "pa") and not (key[0] == "pb" and key[1] % 2 == 0)]
GRP = {key: g for g, key in enumerate(RING)}
for _j in range(0, 8, 2):
    GRP[("pb", _j)] = GRP[("pb", _j + 1)]


def schedule():
    todo = {n: [] for n in range(-1, NB)}

    def put(n, step, *a):
        todo[n].append((step, a))

    put(-1, "x0")
    put(0, "norm", 0)
    for i, kind in enumerate("kqv"):
        for j in range(4):
            n = AT[(kind, j)]
            put(n, "conv4", kind, j)
            put(n + 1, "silu", kind, j)
            if kind != "v":
                put(n + 2, "l2n", kind, j)
    put(3, "ab_mm")
    put(4, "ab_tok")
    put(5, "ab_cum")
    for h in range(0, H1, 2):
        n = 10 + h // 2
        for i in (h, h + 1):
            put(n, "rows", i)
        for i in (h, h + 1):
            put(n + 1, "kk", i)
    for b in range(4):
        put(15 + b // 2, "tok", b)
    put(15, "lev0")
    put(16, "lev0t")
    for l in range(5):
        put(17 + l, "level", l)
    put(22, "uw")
    put(23, "state", 0)
    put(24, "wstate", 1)
    put(25, "state", 1)
    put(26, "wstate", 2)
    put(27, "state", 2)
    put(27, "o", 0)
    put(28, "wstate", 3)
    put(29, "o", 1)
    for q in range(4):
        put(29 + q // 2, "osq", q)
        put(31 + q // 2, "onorm", q)
    for j in range(4):
        n = AT[("x", j)]
        put(n, "gatec", j)
        put(n + 1, "mixc", j)
        put(AT[("ga", j)], "sig", "ga", j)
        n = AT[("gb", j)]
        put(n + 1, "sig", "gb", j)
    for j in range(4):
        n = AT[("z", j)]
        put(n, "zg", j)
        put(AT[("wb", j)], "mix", j)
        put(AT[("wo", j)], "res1", j)
    put(AT[("wb", 0)], "xres")
    put(AT[("wo", 3)], "norm", 1)
    for j in range(FF1):
        n = AT[("u1", j)]
        put(n, "conv3", j)
        put(n + 1, "ffn1", j)
    for q, j in enumerate((8, 9, 10, 10)):
        put(AT[("d1", j)], "res2", q)
    put(AT[("d1", 10)], "norm", 2)
    for kind in ("qa", "ka"):
        for j in range(6):
            n = AT[(kind, j)]
            put(n, "sqh", kind, j)
            put(n + 1, "rmsh", kind, j)
    put(AT[("ka", 0)], "x2")
    put(AT[("qa", 1)], "rtok")
    n = AT[("kr", 0)]
    for i in range(10):
        if i < 8:
            put(n + i, "att_s", i)
        if 1 <= i < 9:
            put(n + i, "att_t", i - 1)
        if i >= 2:
            put(n + i, "att_o", i - 2)
    n = AT[("vr", 2)]
    for h in range(RH):
        put(n + h, "ret_s", h)
    for i in range(8):
        put(AT[("gr", i)] + 1, "silur", i)
    n = AT[("gr", 3)]
    for i in range(9):
        if i < 8:
            put(n + i, "ret_o", i)
        if i:
            put(n + i, "ret_t", i - 1)
    for kind in ("ta", "tb"):
        for j in range(4):
            put(AT[(kind, j)], "sig", kind, j)
    put(AT[("pa", 1)], "ma")
    for j in range(4):
        put(AT[("pb", 2 * j + 1)], "mix2", j)
        put(AT[("w2", j)], "res3", j)
    put(AT[("w2", 3)], "norm", 3)
    for j in range(16):
        put(AT[("u2", j)], "ffn2", j)
    for q in range(4):
        put(AT[("d2", 12 + q)], "res4", q)
    return todo


TODO = schedule()
ORDER = [item for n in range(-1, NB) for item in TODO[n]]
OWN = {"gatec": ("x",), "conv3": ("u1",)}
SIG = {a: i for i, a in enumerate([o[1] for o in ORDER if o[0] == "sig"])}
SILU = {a: i for i, a in enumerate([o[1] for o in ORDER if o[0] == "silu"])}
CONV, TAPS = {}, {}
_n = 0
for _step, _a in ORDER:
    if _step in ("conv4", "gatec", "conv3"):
        _a = OWN.get(_step, ()) + _a
        CONV[_a] = len(CONV)
        _n += 6 if _step == "conv4" else 4
        TAPS[_a] = _n
CONV_KEY = {i: a for a, i in CONV.items()}
HEADN = {a: i for i, (_, a) in enumerate([o for o in ORDER if o[0] in ("l2n", "onorm", "rmsh")])}


SEMS = """
ab abT aba abh abl abv abw am ao as at bag bs bst cum cv cx dec dr dt eg ev f1 f1h f2 f2h fp fq2 fs g2 g2z g3
gc gg gs gtok h h0 hln hsum kb kk kn lt m2 m20 m2h ma mask mc md mm ms ms0 mx mx0 mxh nl nm nsum o oa oah oc
og ogh on or orh out pa_ par pb_ pc pe pn pt qd qk r2 raw0 raw1 rb rd res4 rg ri rl ro row rr rs rsp rt rtT
rtk rtp ry s0 sc sel sg silu sp sq sq0 sqr sr ss ss0 ssa st t0 t0c tap tb tk tok tsa uw uwp vn wh wl ws x0 x0h
x1 x1h x2 x3 x3h xT xb xbh xres ya yah zp zs
""".split()


def program(nc, wts, par_d, x_d, abw_d, sums_d, mask_d, sel_d, md_d, dr_d, out_d):
    with ExitStack() as ctx:
        def sb(name, shape, dt=F32, own=None):
            return (own or ctx).enter_context(nc.sbuf_tensor(name, shape, dt))

        sem = {name: ctx.enter_context(nc.semaphore("s_" + name)) for name in SEMS}
        raw = sb("raw", [P, 2, 16, P])
        wh = sb("wh", [P, 3, 16, P], F32R)
        wl = sb("wl", [P, 3, 16, P], F32R)
        Yh, Yl = sb("Yh", [P, KT, S], F32R), sb("Yl", [P, KT, S], F32R)
        xT = sb("xT", [P, KT, S])
        par = sb("par", [P, NPAR])
        rb, rfin, lnt = sb("rb", [P, S]), sb("rfin", [P, S]), sb("lnt", [P, S])
        y = [sb(f"y{i}", [P, 2, S]) for i in range(2)]
        acc = [sb(f"acc{i}", [P, 2, S]) for i in range(2)]
        e = [sb(f"e{i}", [P, 2, S]) for i in range(2)]
        t2 = [sb(f"t2{i}", [P, 2, S]) for i in range(2)]
        sq = [sb(f"sq{i}", [P, 2, S]) for i in range(2)]
        ss = [sb(f"ss{i}", [P, 2, S]) for i in range(2)]
        small = sb("small", [P, 64])
        rtok = sb("rtok", [P, 2])
        with ExitStack() as own:
            Xh, Xl = sb("Xh", [P, KT, S], F32R, own), sb("Xl", [P, KT, S], F32R, own)
        xf = sb("xf", [P, 4096])
        dr = xf[:, 2048:3072].rearrange("p (h i) -> p h i", h=4)
        md = xf[:, 3072:3840].rearrange("p (g i) -> p g i", g=3)
        ST = [xf[:, a:a + 384] for a in (0, 384, 1024, 1408)]
        with ExitStack() as own:
            ga_ = sb("gdn", [P, 8, KT, S], F32, own)
        with ExitStack() as own:
            sb("below", [P, 4, KT, S], F32, own)
            abh, abl = sb("abh", [P, KT, 64], F32R, own), sb("abl", [P, KT, 64], F32R, own)
        with ExitStack() as own:
            Zh, Zl = sb("Zh", [P, KT, S], F32R, own), sb("Zl", [P, KT, S], F32R, own)
        sc = sb("mix2", [P, 16384])
        with ExitStack() as own:
            cg, bg = sb("cg", [P, 2, S], F32, own), sb("bg", [P, 2, S], F32, own)
            G2, abt = sb("G2", [64, S], F32, own), sb("abt", [64, 3, S], F32, own)
        Oh, Ol = sb("Oh", [P, 4, S], F32R), sb("Ol", [P, 4, S], F32R)

        def full(i):
            return ga_[:, i]

        def tiles(i):
            return ga_[:, i].rearrange("p h (t m) -> p h t m", t=2)

        qn, kn, vv, kb, qd, DT, LT, AQ = (full(i) for i in range(8))
        SI, KD, VB, TI, KBE, U, WT, OT = (tiles(0), tiles(1), tiles(2), tiles(3), tiles(5), tiles(6), tiles(3), full(5))
        sgb, xres = full(0), full(3)
        hist = [ga_[:, 0, 0:4].rearrange("p a (b m) -> p (a b) m", b=2),
                ga_[:, 0, 4:8].rearrange("p a (b m) -> p (a b) m", b=2),
                ga_[:, 2, 0:4].rearrange("p a (b m) -> p (a b) m", b=2)]
        dec = ga_[:, 2, 4:8].rearrange("p a (b m) -> p (a b) m", b=2)
        m1 = xT
        sel = xT[:, 0:4].rearrange("p a (b m) -> p (a b) m", b=2)
        sums = xT[:, 5:8].rearrange("p a (b m) -> p (a b) m", b=2)[:, 0:5]
        negm, tri, blk, cm = sums[:, 0], sums[:, 1], sums[:, 2], (sums[:, 3], sums[:, 4])
        mask = xT[:, 0:3].rearrange("p a (b m) -> p (a b) m", b=2)
        abw = ga_[:, 5, 0:2].rearrange("p a (b m) -> p (a b) m", b=4)
        atn = sb("atn", [P, 2, 4])
        bst, bag, rsd = sb("bst", [P, 2, 6]), sb("bag", [P, 2, 2]), sb("rsd", [P, 2, 2])
        G3 = xT[0:8, 4]
        gtok = sb("gtok", [P, 2, 40])
        TS = sb("TS", [P, 5, H1, 2])
        egl = sb("egl", [P, 4, H1])
        Gs = sb("Gs", [P, 64])

        def part(kb_, n, **kw):
            return sc[:, 256 * kb_:256 * (kb_ + n)].rearrange("p (a i) -> p a i", **kw)

        att_s = [part(3 * i, 3, a=3) for i in range(2)]
        att_p = [part(6 + 3 * i, 3, a=6) for i in range(2)]
        qr, qa, ka, kr = part(12, 8, a=8), part(20, 12, a=12), part(32, 12, a=12), part(56, 8, a=8)
        va = part(44, 12, a=2)
        vr = part(20, 16, a=2)
        gr = part(36, 16, a=16)
        ta = part(52, 8, a=8)

        def tb(j):
            return part(60 + 2 * j, 2, a=2) if j < 2 else part(12 + 2 * j, 2, a=2)

        psS = [ctx.enter_context(nc.psum_tensor(f"psS{i}", [P, 2, S], F32)) for i in range(2)]
        psA = [ctx.enter_context(nc.psum_tensor(f"psA{i}", [P, 2, S], F32)) for i in range(6)]

        def flat(b):
            return psA[b][:].rearrange("p a b -> p (a b)")

        def quad(b):
            return psA[b][:].rearrange("p a (c m) -> p (a c) m", m=P)

        def pcol(name, i=0, lo=0, hi=P):
            return par[lo:hi, PAR[name] + i:PAR[name] + i + 1]

        ident = par[:, PAR["ident"]:PAR["ident"] + P]
        ones = par[:, PAR["ones"]:PAR["ones"] + P]
        gg = small[:, 0:8]

        def two(ap):
            return ap.unsqueeze(1).broadcast_to([P, 2, S])

        def f32(ap):
            return ap.bitcast(F32)

        def ring(key):
            return psS[GRP[key] % 2]

        def pair(t, j):
            return t[:, 2 * j:2 * j + 2]

        GDST = {"ta": lambda j: pair(ta, j), "tb": tb, "gb": lambda j: pair(sgb, j)}
        QK = {"qa": qa, "ka": ka}
        QKV = {"q": qn, "k": kn, "v": vv}
        YKINDS = ("k", "q", "v", "x", "ga", "gb", "z", "u1", "gr", "ta", "tb")

        def yk(key):
            return y[AT[key] % 2]

        def hbank(i):
            return psA[2 + i % 2] if i < 8 else psA[i % 2]

        block = ctx.enter_context(nc.Block())

        @block.sync
        def _(sp):
            sp.dma_start(par[:], par_d).then_inc(sem["par"], 16)
            sp.dma_start(xT[:], x_d).then_inc(sem["xT"], 16)

            def load(n):
                if n >= 2:
                    sp.wait_ge(sem["wl"], n - 1)
                sp.dma_start(raw[:, n % 2], wts[n]).then_inc(sem[f"raw{n % 2}"], 16)

            load(0)
            load(1)
            sp.dma_start(abw, abw_d).then_inc(sem["abw"], 16)
            for n in range(2, NB):
                load(n)
                if n == 3:
                    sp.wait_ge(sem["ss"], 1)
                    sp.wait_ge(sem["x0"], KT)
                    sp.dma_start(sel, sel_d).then_inc(sem["sel"], 16)
                    sp.dma_start(sums, sums_d).then_inc(sem["gc"], 16)
                if n == AT[("c", 1)]:
                    sp.wait_ge(sem["row"], 8)
                    sp.dma_start(mask, mask_d).then_inc(sem["mask"], 16)
                if n == AT[("wb", 2)]:
                    sp.wait_ge(sem["vn"], 6)
                    sp.dma_start(xres, x_d).then_inc(sem["xres"], 16)
                if n == AT[("ka", 0)]:
                    sp.wait_ge(sem["mm"], AT[("d1", 10)] + 1)
                    sp.dma_start(xf[:, 2048:3072], dr_d).then_inc(sem["dr"], 16)
                    sp.dma_start(xf[:, 3072:3840], md_d).then_inc(sem["md"], 16)
            for q in range(4):
                sp.wait_ge(sem["res4"], q + 1)
                sp.dma_start(pair(out_d, q), pair(xT, q)).then_inc(sem["out"], 16)
            sp.wait_ge(sem["out"], 64)

        @block.tensor
        def _(pe):
            OPER = {}
            for kind in COL1:
                OPER[kind] = (Xh, Xl, "x0", lambda k: k + 1)
            OPER["ga"] = OPER["gb"] = OPER["x"]
            OPER["wa"] = (Yh, Yl, "ya", lambda k: k // 2 + 1)
            OPER["wb"] = (Yh, Yl, "og", lambda k: k // 2 + 1)
            OPER["wo"] = (Xh, Xl, "mx", lambda k: k // 2 + 1)
            OPER["u1"] = (Yh, Yl, "x1", lambda k: k + 1)
            for kind in COL2:
                OPER[kind] = (Yh, Yl, "xb", lambda k: k + 1)
            OPER["w2"] = (Yh, Yl, "m2", lambda k: k // 2 + 1)
            OPER["u2"] = (Xh, Xl, "x3", lambda k: k + 1)

            def operand(kind, k):
                if kind == "d1":
                    h, l = ((Xh, Xl), (Zh, Zl), (Xh, Xl))[k // 8]
                    return h, l, k % 8, "f1", k + 1
                if kind == "d2":
                    h, l = ((Yh, Yl), (Zh, Zl))[k // 8 % 2]
                    return h, l, k % 8, "f2", k // 2 + 1
                if kind == "pa":
                    return Oh, Ol, k, "oa", 8
                if kind == "pb":
                    h, l = ((Zh, Zl), (Xh, Xl))[k // 8]
                    return h, l, k % 8, "or", 2 * (k // 4) + 2
                h, l, s, v = OPER[kind]
                return h, l, k, s, v(k)

            def stream(n):
                kind, j = SEQ[n]
                pe.wait_ge(sem["wl"], n + 1)
                key = (kind, j)
                fresh = True
                if key in RING or kind == "pb":
                    fresh = not (kind == "pb" and j % 2)
                    if fresh and GRP[key] >= 2:
                        pe.wait_ge(sem["ev"], GRP[key] - 1)
                if kind == "pa":
                    pe.wait_ge(sem["rt"], 8)
                if kind == "d2" and j == 0:
                    pe.wait_ge(sem["ma"], 4)
                if kind == "d1" and j == 0:
                    pe.wait_ge(sem["og"], 4)
                _, prs = pairs(kind, j)
                seen = set()
                begun = set()
                for p, (k, c) in enumerate(prs):
                    h, l, kk_, s, v = operand(kind, k)
                    if k not in seen:
                        pe.wait_ge(sem[s], v)
                        seen.add(k)
                    if kind in ("va", "vr"):
                        if p % 2:
                            continue
                        w = [t[:, n % 3].rearrange("p a b -> p (a b)")[:, p * P:(p + 2) * P] for t in (wh, wl)]
                        for t in range(2):
                            o = ring(key)[:, t]
                            for i, (a, b) in enumerate(((h, w[0]), (l, w[0]), (h, w[1]))):
                                mm = pe.matmul(o, a[:, kk_, t * P:(t + 1) * P], b,
                                               start=(p == 0 and t == 0 and i == 0), stop=(p == 14 and i == 2),
                                               skip_group_check=True)
                        continue
                    if kind in ("d1", "d2", "pa"):
                        bank, half = psA[c // 2], c % 2
                    else:
                        bank, half = ring(key), p % 2
                    first = {"d1": k == 0 and c % 2 == 0, "d2": k == 0 and c % 2 == 0,
                             "pa": k == 0 and c % 2 == 0}.get(kind, fresh and p == 0)
                    last = {"d1": k == FF1 - 1, "d2": k == 31, "pa": k == 3,
                            "pb": j % 2 == 1 and p >= 14}.get(kind, p >= 14)
                    for i, (a, b) in enumerate(((wh, h), (wh, l), (wl, h))):
                        mm = pe.matmul(bank[:, half], a[:, n % 3, p, :], b[:, kk_, :], start=(first and i == 0),
                                       stop=(last and i == 2), skip_group_check=True)
                mm.then_inc(sem["mm"], 1)

            def norm(i):
                pe.wait_ge(sem["ss"], i + 1)
                if i:
                    pe.wait_ge(sem["rb"], i)
                for g in range(2 if i == 2 else 1):
                    for half in range(2):
                        mm = pe.matmul(psA[5][:, g], ones, ss[g][:, half], start=(half == 0), stop=(half == 1),
                                       skip_group_check=True)
                mm.then_inc(sem["nsum"], 1)

            def ab_mm():
                pe.wait_ge(sem["abl"], 1)
                for k in range(KT):
                    for i, (a, b) in enumerate(((abh, Xh), (abh, Xl), (abl, Xh))):
                        mm = pe.matmul(psA[4][0:64, 0], a[:, k], b[:, k], start=(k == 0 and i == 0),
                                       stop=(k == KT - 1 and i == 2))
                mm.then_inc(sem["ab"], 1)

            def ab_tok():
                pe.wait_ge(sem["g2"], 2)
                for t in range(2):
                    mm = pe.transpose(psA[4][:, 0, 40 * t:40 * t + 40], G2[0:40, t * P:(t + 1) * P],
                                      ident[0:40, 0:40])
                mm.then_inc(sem["abT"], 1)

            def ab_cum():
                pe.wait_ge(sem["gtok"], 1)
                pe.wait_ge(sem["gc"], 16)
                q = flat(4)
                for t in range(2):
                    g = gtok[:, t, 0:8]
                    outs = ((tri, 8 * t), (blk, 16 + 8 * t), (cm[0], 32 + 16 * t), (cm[1], 40 + 16 * t))
                    for a, o in outs:
                        pe.matmul(q[:, o:o + 8], a, g, start=True, stop=True)
                for t in range(2):
                    mm = pe.matmul(psA[4][0:8, 1, t * P:(t + 1) * P], gtok[:, t, 0:8], tri, start=True, stop=True)
                mm.then_inc(sem["cum"], 1)

            def colsum(i, bank, src, count):
                pe.wait_ge(sem["sq"], count)
                pe.matmul(psA[bank][:], ones, src, start=True, stop=True).then_inc(sem["hsum"], 1)

            def l2n(kind, j):
                i = HEADN[(kind, j)]
                if i >= 2:
                    pe.wait_ge(sem["hln"], i - 1)
                colsum(i, 2 + i % 2, sq[i % 2][:], i + 1)

            def onorm(q):
                i = HEADN[(q,)]
                if q < 2:
                    pe.wait_ge(sem["vn"], 6)
                pe.wait_ge(sem["hln"], i - 1)
                colsum(i, q % 2, sq[i % 2][:], i + 1)

            def rmsh(kind, j):
                i = HEADN[(kind, j)]
                pe.wait_ge(sem["hln"], i - 1)
                if i == 12:
                    pe.wait_ge(sem["xb"], 8)
                colsum(i, i % 2, sq[i % 2][:], i + 1)

            def rows(h):
                if h == 0:
                    pe.wait_ge(sem["sel"], 16)
                    pe.wait_ge(sem["g3"], 1)
                if h >= 2:
                    pe.wait_ge(sem["eg"], h - 1)
                pe.matmul(psA[4 * (h % 2)][:, 0], sel[32:40, h], G2[32:40, :], start=True, stop=True)
                pe.matmul(psA[4 * (h % 2) + 1][:, 1], sel[0:8, h], G3, start=True, stop=True).then_inc(sem["row"], 1)

            def kk(h):
                if h == 0:
                    pe.wait_ge(sem["kn"], 8)
                    pe.wait_ge(sem["hln"], 8)
                pe.wait_ge(sem["kb"], 2 * h + 1)
                if h >= 2:
                    pe.wait_ge(sem["lt"], 2 * h - 2)
                for t in range(2):
                    s = slice(t * P, (t + 1) * P)
                    pe.matmul(quad(2 + h % 2)[:, 2 * t], kn[:, h, s], kb[:, h, s], start=True, stop=True)
                    mm = pe.matmul(quad(2 + h % 2)[:, 2 * t + 1], kn[:, h, s], qn[:, h, s], start=True, stop=True)
                mm.then_inc(sem["kk"], 1)

            def tok(b):
                if b == 0:
                    pe.wait_ge(sem["silu"], 12)
                    pe.wait_ge(sem["eg"], 8)
                if b:
                    pe.wait_ge(sem["tok"], 3 * b)
                for src, bank in ((kn, 4), (vv, 5)):
                    for i in range(4):
                        mm = pe.transpose(quad(bank)[:, i], src[:, 2 * b + i // 2, i % 2 * P:(i % 2 + 1) * P], ident)
                    mm.then_inc(sem["tk"], 1)

            def lev0t():
                pe.wait_ge(sem["eg"], 8)
                pe.wait_ge(sem["lt"], 16)
                for b in range(4):
                    pe.wait_ge(sem["s0"], 2 * b + 2)
                    for i in range(4):
                        mm = pe.transpose(quad(b)[:, i], SI[:, 2 * b + i // 2, i % 2], ident)
                    mm.then_inc(sem["t0"], 1)

            def level(l):
                def left(b):
                    i = 4 * l + b
                    pe.wait_ge(sem["bs"], i + 1)
                    if l == 0:
                        pe.wait_ge(sem["t0c"], b + 1)
                        if b < 2:
                            pe.wait_ge(sem["tok"], 12)
                    else:
                        pe.wait_ge(sem["st"], 2 * (i - 4) + 2)
                    if i >= 2:
                        pe.wait_ge(sem["pc"], i - 1)
                    for q in range(4):
                        mm = pe.matmul(quad(4 + b % 2)[:, q], sq[b % 2][:].rearrange("p a (c m) -> p (a c) m", m=P)[:, q],
                                       TI[:, 2 * b + q // 2, q % 2], start=True, stop=True)
                    mm.then_inc(sem["pa_"], 1)

                def right(b):
                    i = 4 * l + b
                    pe.wait_ge(sem["pc"], i + 1)
                    if l == 0:
                        pe.wait_ge(sem["t0c"], 4)
                    if i >= 2:
                        pe.wait_ge(sem["st"], 2 * (i - 2) + 2 if i - 2 < 16 else 32 + i - 17)
                    pb = ss[b % 2][:].rearrange("p a (c m) -> p (a c) m", m=P)
                    for q in range(4):
                        s = SI[:, 2 * b + q // 2, q % 2]
                        mm = pe.matmul(quad(2 * (b % 2))[:, q], pb[:, q], s, start=True, stop=True)
                    if l < 4:
                        for q in range(4):
                            s = SI[:, 2 * b + q // 2, q % 2]
                            mm = pe.matmul(quad(2 * (b % 2) + 1)[:, q], s, pb[:, q], start=True, stop=True)
                    mm.then_inc(sem["pb_"], 1)

                left(0)
                left(1)
                right(0)
                left(2)
                right(1)
                left(3)
                right(2)
                right(3)

            def uw():
                for b in range(4):
                    pe.wait_ge(sem["st"], 32 + (4 if b < 2 else b + 1))
                    if b >= 2:
                        pe.wait_ge(sem["uw"], 2 * (b - 2) + 2)
                    for q in range(4):
                        mm = pe.matmul(quad(2 * (b % 2))[:, q], SI[:, 2 * b + q // 2, q % 2],
                                       VB[:, 2 * b + q // 2, q % 2], start=True, stop=True)
                    for q in range(4):
                        mm = pe.matmul(quad(2 * (b % 2) + 1)[:, q], KBE[:, 2 * b + q // 2, q % 2],
                                       SI[:, 2 * b + q // 2, q % 2], start=True, stop=True)
                    mm.then_inc(sem["uwp"], 1)

            def state(c):
                t, r = c // 2, slice(CHUNK * (c % 2), CHUNK * (c % 2) + CHUNK)
                if c == 0:
                    pe.wait_ge(sem["uw"], 8)
                    pe.wait_ge(sem["pc"], 20)
                else:
                    pe.wait_ge(sem["vn"], 2 * c)
                    pe.wait_ge(sem["h0"], 2) if c == 1 else pe.wait_ge(sem["h"], 2 * c - 2)
                for h in range(H1):
                    mm = pe.matmul(quad(4 + h // 4)[:, h % 4], KD[r, h, t], U[r, h, t], start=True, stop=True)
                mm.then_inc(sem["sp"], 1)

            def wstate(c):
                t = c // 2
                pe.wait_ge(sem["h0"], 2) if c == 1 else pe.wait_ge(sem["h"], 2 * c - 2)
                if c > 1:
                    pe.wait_ge(sem["vn"], 2 * c - 2)
                for h in range(H1):
                    mm = pe.matmul(quad(h // 4)[:, h % 4], WT[:, h, t], hist[c - 1][:, h], start=True, stop=True)
                mm.then_inc(sem["ws"], 1)

            def o(t):
                pe.wait_ge(sem["vn"], 4 * t + 2)
                pe.wait_ge(sem["h"], 4 * t) if t else pe.wait_ge(sem["h0"], 2)
                if t:
                    pe.wait_ge(sem["oc"], 2)
                for h in range(H1):
                    dst = quad(2 + h // 4)[:, h % 4]
                    mm = pe.matmul(dst, U[:, h, t], AQ[:, h, t * P:(t + 1) * P], start=True, stop=False,
                                   skip_group_check=True)
                    for c in (2 * t, 2 * t + 1):
                        if c:
                            lo = CHUNK * (c % 2)
                            mm = pe.matmul(dst[:, lo:lo + CHUNK], hist[c - 1][:, h],
                                           qd[:, h, c * CHUNK:(c + 1) * CHUNK], start=False,
                                           stop=(c % 2 == 1), skip_group_check=True)
                    if h % 4 == 3:
                        mm.then_inc(sem["o"], 1)

            def rtok_():
                pe.wait_ge(sem["rb"], 3)
                for t in range(2):
                    mm = pe.matmul(flat(4)[:, t:t + 1], rb[0:1, t * P:(t + 1) * P], ones[0:1, 0:1],
                                   start=True, stop=True)
                mm.then_inc(sem["rtp"], 1)

            def att_s_(i):
                hp, t = i // 2, i % 2
                n = P * (t + 1)
                if i == 0:
                    pe.wait_ge(sem["qk"], 24)
                if i >= 2:
                    pe.wait_ge(sem["sc"], 3 * (i - 1))
                for g in range(3):
                    h = 4 * g + hp
                    dst = flat(0)[:, g * P:(g + 1) * P] if t == 0 else psA[2 + g // 2][:, g % 2]
                    mm = pe.matmul(dst, qa[:, h, t * P:(t + 1) * P], ka[:, h, 0:n], start=True, stop=True)
                mm.then_inc(sem["as"], 1)

            def att_t(i):
                t = i % 2
                pe.wait_ge(sem["pn"], i + 1)
                if i:
                    pe.wait_ge(sem["pt"], i)
                for g in range(3):
                    for jt in range(t + 1):
                        q = g * (t + 1) + jt
                        mm = pe.transpose(quad(4 + q // 4)[:, q % 4], att_s[i % 2].rearrange("p a (c m) -> p (a c) m", m=P)[:, q], ident)
                mm.then_inc(sem["at"], 1)

            def att_o(i):
                hp, t = i // 2, i % 2
                pe.wait_ge(sem["pt"], i + 1)
                if i:
                    pe.wait_ge(sem["oa"], i)
                n = 3 * (t + 1)
                for q in range(n):
                    g, jt = q // (t + 1), q % (t + 1)
                    h = 4 * g + hp
                    mm = pe.matmul(quad(1)[:, 0], va[:, jt, h * P:(h + 1) * P], att_p[i % 2][:, q],
                                   start=(q == 0), stop=(q == n - 1))
                mm.then_inc(sem["ao"], 1)

            def ret_s(h):
                if h == 0:
                    pe.wait_ge(sem["sc"], 24)
                if h >= 2:
                    pe.wait_ge(sem["rs"], 2 * h - 2)
                b = 2 * (h % 2)
                for a in range(2):
                    pe.matmul(psA[b][:, 0], kr[:, 2 * h + a, 0:P], qr[:, 2 * h + a, :], start=(a == 0), stop=(a == 1))
                for a in range(2):
                    mm = pe.matmul(psA[b][:, 1, 0:P], kr[:, 2 * h + a, P:S], qr[:, 2 * h + a, P:S],
                                   start=(a == 0), stop=(a == 1))
                mm.then_inc(sem["rsp"], 1)

            def ret_o(i):
                h, t = i // 2, i % 2
                if i == 0:
                    pe.wait_ge(sem["rs"], 8)
                    pe.wait_ge(sem["pt"], 8)
                if i >= 2:
                    pe.wait_ge(sem["ry"], i - 1)
                for a in range(t + 1):
                    lhs = ST[h][:, t * P:(t + 1) * P] if a == 0 else ST[h][:, 2 * P:3 * P]
                    mm = pe.matmul(psA[4 + i % 2][:], lhs, vr[:, a, h * 512:(h + 1) * 512], start=(a == 0), stop=(a == t))
                mm.then_inc(sem["ro"], 1)

            def ret_t(i):
                pe.wait_ge(sem["ry"], i + 1)
                if i >= 2:
                    pe.wait_ge(sem["rt"], i - 1)
                if i < 2:
                    pe.wait_ge(sem["oa"], 8)
                for f in range(4):
                    mm = pe.transpose(quad(i % 2)[:, f], acc[i % 2][:].rearrange("p a (c m) -> p (a c) m", m=P)[:, f],
                                      ident)
                mm.then_inc(sem["rtT"], 1)

            steps = {"norm": norm, "ab_mm": ab_mm, "ab_tok": ab_tok, "ab_cum": ab_cum, "l2n": l2n, "onorm": onorm,
                     "rmsh": rmsh, "rows": rows, "kk": kk, "tok": tok, "lev0t": lev0t, "level": level, "uw": uw,
                     "state": state, "wstate": wstate, "o": o, "rtok": rtok_, "att_s": att_s_, "att_t": att_t,
                     "att_o": att_o, "ret_s": ret_s, "ret_o": ret_o, "ret_t": ret_t}
            pe.wait_ge(sem["par"], 16)
            for n in range(NB):
                stream(n)
                for step, a in TODO[n]:
                    if step in steps:
                        steps[step](*a)

        @block.scalar
        def _(act):
            def split(n):
                act.wait_ge(sem[f"raw{n % 2}"], 16 * (n // 2 + 1))
                if n >= 3:
                    act.wait_ge(sem["mm"], n - 2)
                act.activation(wh[:, n % 3], raw[:, n % 2], ACT.Copy).then_inc(sem["wh"], 1)

            def high(dst, src, scale, name):
                act.activation(dst, src, ACT.Copy, scale=scale).then_inc(sem[name], 1)

            def x0():
                act.wait_ge(sem["par"], 16)
                act.wait_ge(sem["xT"], 16)
                for k in range(KT):
                    high(Xh[:, k], xT[:, k], pcol("g_mix", k), "x0h")

            def norm(i):
                act.wait_ge(sem["nsum"], i + 1)
                if i:
                    act.wait_ge(sem["rb"], i)
                act.activation(lnt[:], psA[5][:, 0], ACT.Ln, bias=pcol("eps"), scale=1.0 / D).then_inc(sem["nl"], 1)
                n = {0: 1, 1: 2, 2: 3, 3: 7}[i]
                act.wait_ge(sem["nl"], n)
                if i != 2:
                    if i:
                        act.wait_ge(sem["ev"], GRP[{1: ("wo", 3), 3: ("w2", 3)}[i]] + 1)
                    act.activation(rb[:], lnt[:], ACT.Exp, scale=-0.5).then_inc(sem["rb"], 1)
                    return
                act.activation(rfin[:], lnt[:], ACT.Exp, scale=-0.5).then_inc(sem["nl"], 1)
                act.wait_ge(sem["ms"], 1)
                act.activation(lnt[:], lnt[:], ACT.Ln, bias=pcol("eps"), scale=1.0 / D).then_inc(sem["nl"], 1)
                act.wait_ge(sem["nl"], 5)
                act.activation(lnt[:], lnt[:], ACT.Exp, scale=-0.5).then_inc(sem["nl"], 1)

            def taps(a, w):
                i = CONV[a]
                if i >= 2:
                    b = CONV_KEY[i - 2]
                    if b[0] in QKV:
                        act.wait_ge(sem["silu"], SILU[b] + 1)
                    else:
                        act.wait_ge(sem["mc" if b[0] == "x" else "fp"], b[1] + 1)
                for f in range(2):
                    t = act.activation(acc[i % 2][:, f], yk(a)[:, f], ACT.Copy, scale=w[f])
                t.then_inc(sem["tap"], 1)

            def conv4(kind, j):
                act.wait_ge(sem["ev"], GRP[(kind, j)] + 1)
                c = {"q": 0, "k": 8, "v": 16}[kind] + 2 * j
                taps((kind, j), [pcol("conv_g", 72 + c + f) for f in range(2)])

            def gatec(j):
                act.wait_ge(sem["cx"], j + 1)
                taps(("x", j), [pcol("conv_a", 16 + 2 * j + f) for f in range(2)])

            def conv3(j):
                act.wait_ge(sem["ev"], GRP[("u1", j)] + 1)
                taps(("u1", j), [pcol("conv_f", 2 * 2 * FF1 + j + f * FF1) for f in range(2)])

            def silu(kind, j):
                act.wait_ge(sem["cv"], TAPS[(kind, j)])
                act.activation(pair(QKV[kind], j), acc[CONV[(kind, j)] % 2][:], ACT.Silu).then_inc(sem["silu"], 1)

            def sig(kind, j):
                act.wait_ge(sem["ev"], GRP[(kind, j)] + 1)
                if kind == "ga":
                    if j >= 2:
                        act.wait_ge(sem["ev"], GRP[("wa", j - 2)] + 1)
                    dst = e[j % 2][:]
                else:
                    dst = GDST[kind](j)
                act.activation(dst, yk((kind, j))[:], ACT.Sigmoid).then_inc(sem["sg"], 1)

            def zg(j):
                act.wait_ge(sem["ev"], GRP[("z", j)] + 1)
                if j >= 2:
                    act.wait_ge(sem["zp"], j - 1)
                act.activation(e[j % 2][:], yk(("z", j))[:], ACT.Silu).then_inc(sem["zs"], 1)
                act.wait_ge(sem["zp"], j + 1)
                high(pair(Yh, j), t2[j % 2][:], 1.0, "ogh")

            def silur(j):
                act.wait_ge(sem["ev"], GRP[("gr", j)] + 1)
                act.activation(pair(gr, j), yk(("gr", j))[:], ACT.Silu).then_inc(sem["sr"], 1)

            def ffn1(j):
                act.wait_ge(sem["cv"], TAPS[("u1", j)])
                if j >= 2:
                    act.wait_ge(sem["fp"], j - 1)
                act.activation(e[j % 2][:, 0], acc[CONV[("u1", j)] % 2][:, 0], ACT.Silu).then_inc(sem["fs"], 1)
                act.wait_ge(sem["fp"], j + 1)
                high(((Xh, Zh, Xh)[j // 8])[:, j % 8], t2[j % 2][:, 1], 1.0, "f1h")

            def headnorm(i, scale, bias):
                act.wait_ge(sem["hsum"], i + 1)
                act.activation(t2[i % 2][:], hbank(i)[:], ACT.Ln, bias=pcol("eps"), scale=scale).then_inc(sem["hln"], 1)
                act.wait_ge(sem["hln"], i + 1)
                act.activation(t2[i % 2][:], t2[i % 2][:], ACT.Exp, scale=-0.5, bias=bias).then_inc(sem["ri"], 1)

            def l2n(kind, j):
                i = HEADN[(kind, j)]
                if i >= 2:
                    act.wait_ge(sem["kn"], i - 1)
                headnorm(i, 1.0, pcol("ln_scale") if kind == "q" else 0.0)

            def ab_mm():
                act.wait_ge(sem["abv"], 3)
                act.activation(abt[0:8, 0], abt[0:8, 2], ACT.Exp, scale=-1.0).then_inc(sem["aba"], 1)
                act.activation(abt[32:40, 1], abt[32:40, 0], ACT.Exp, scale=-1.0).then_inc(sem["aba"], 1)
                act.activation(small[0:8, 8:9], pcol("a_log", hi=8), ACT.Exp).then_inc(sem["aba"], 1)
                act.wait_ge(sem["abv"], 4)
                act.activation(abt[8 - 8:8, 2], G3, ACT.Ln).then_inc(sem["aba"], 1)

            def ab_cum():
                act.wait_ge(sem["gs"], 3)
                act.activation(TS[:, 4].rearrange("p h t -> p t h"), Gs[:, 0:16].rearrange("p (t h) -> p t h", t=2),
                               ACT.Exp).then_inc(sem["tsa"], 1)
                act.activation(TS[:, 3], TS[:, 3], ACT.Exp).then_inc(sem["tsa"], 1)
                act.activation(egl[:], Gs[:, 32:64].rearrange("p (c h) -> p c h", c=4), ACT.Exp).then_inc(sem["tsa"], 1)

            def rows(h):
                act.wait_ge(sem["kb"], 2 * h + 2)
                act.wait_ge(sem["kn"], 8) if h < 2 else act.wait_ge(sem["qd"], h - 1)
                act.activation(t2[h % 2][:, 0], psA[4 * (h % 2) + 1][:, 1], ACT.Exp).then_inc(sem["eg"], 1)
                if h == 0:
                    act.wait_ge(sem["gs"], 3)
                for t in range(2):
                    s = slice(t * P, (t + 1) * P)
                    a = act.activation(DT[:, h, s], DT[:, h, s], ACT.Exp, bias=TS[:, 0, h, t:t + 1])
                a.then_inc(sem["dt"], 1)

            def mixc(j):
                act.wait_ge(sem["mc"], j + 1)
                high(pair(Yh, j), t2[j % 2][:], 1.0, "yah")

            def lev0t():
                for b in range(4):
                    act.wait_ge(sem["t0"], b + 1)
                    act.activation(TI[:, 2 * b:2 * b + 2], psA[b][:].rearrange("p a (c m) -> p a c m", m=P),
                                   ACT.Copy).then_inc(sem["t0c"], 1)

            def level(l):
                for b in range(4):
                    i = 4 * l + b
                    act.wait_ge(sem["pa_"], i + 1)
                    if i >= 2:
                        act.wait_ge(sem["pb_"], i - 1)
                    act.activation(ss[b % 2][:], psA[4 + b % 2][:], ACT.Copy).then_inc(sem["pc"], 1)

            def uw():
                for b in range(4):
                    act.wait_ge(sem["uwp"], b + 1)
                    for i, dst in enumerate((U, WT)):
                        act.activation(dst[:, 2 * b:2 * b + 2],
                                       psA[2 * (b % 2) + i][:].rearrange("p a (c m) -> p a c m", m=P),
                                       ACT.Copy).then_inc(sem["uw"], 1)

            def state(c):
                if c == 0:
                    act.wait_ge(sem["sp"], 1)
                    for q in range(2):
                        act.activation(hist[0][:, 4 * q:4 * q + 4], quad(4 + q), ACT.Copy).then_inc(sem["h0"], 1)

            def o(t):
                for q in range(2):
                    act.wait_ge(sem["o"], 2 * t + q + 1)
                    act.activation(OT[:, 4 * q:4 * q + 4, t * P:(t + 1) * P], quad(2 + q), ACT.Copy).then_inc(sem["oc"], 1)

            def onorm(q):
                act.wait_ge(sem["on"], q - 1) if q >= 2 else act.wait_ge(sem["ya"], 4)
                headnorm(HEADN[(q,)], 1.0 / P, 0.0)

            def mix(j):
                act.wait_ge(sem["mx0"], j + 1)
                high(pair(Xh, j), t2[j % 2][:], 1.0, "mxh")

            def squares(i, j, gain):
                base = {1: 0, 2: 3, 3: 10}[i]
                per = 2 if i == 2 else 1
                if j >= 2:
                    act.wait_ge(sem["ssa"], base + per * (j - 1))
                act.activation(sq[j % 2][:], pair(xT, j), ACT.Square).then_inc(sem["sqr"], 1)
                if i == 2:
                    for f in range(2):
                        a = act.activation(t2[j % 2][:, f], xT[:, 2 * j + f], ACT.Square, scale=pcol("g_fin", 2 * j + f))
                    a.then_inc(sem["sqr"], 1)

            def res1(j):
                act.wait_ge(sem["ev"], GRP[("wo", j)] + 1)
                for k in (2 * j, 2 * j + 1):
                    high(Yh[:, k], xT[:, k], pcol("g_ffn", k), "x1h")
                squares(1, j, None)

            def res2(j):
                act.wait_ge(sem["r2"], j + 1)
                for k in (2 * j, 2 * j + 1):
                    high(Yh[:, k], xT[:, k], gg[:, k:k + 1], "xbh")
                squares(2, j, None)

            def res3(j):
                act.wait_ge(sem["ev"], GRP[("w2", j)] + 1)
                for k in (2 * j, 2 * j + 1):
                    high(Xh[:, k], xT[:, k], pcol("g_n2", k), "x3h")
                squares(3, j, None)

            def sqh(kind, j):
                act.wait_ge(sem["ev"], GRP[(kind, j)] + 1)
                i = HEADN[(kind, j)]
                act.wait_ge(sem["hsum"], i - 1)
                if i == 12:
                    act.wait_ge(sem["ss"], 3)
                act.activation(sq[i % 2][:], pair(QK[kind], j), ACT.Square).then_inc(sem["sq"], 1)

            def rmsh(kind, j):
                i = HEADN[(kind, j)]
                if i == 12:
                    act.wait_ge(sem["ss"], 3)
                act.wait_ge(sem["qk"], 2 * (i - 12) - 2) if i >= 14 else None
                headnorm(i, 1.0 / P, 0.0)

            def att_s_(i):
                act.wait_ge(sem["nm"], i + 1)
                n = 3 * P * (i % 2 + 1)
                v = att_s[i % 2].rearrange("p a b -> p (a b)")[:, 0:n]
                act.activation(v, v, ACT.Exp, scale=SCALE, bias=atn[:, i % 2, 1:2],
                               accum_out=atn[:, i % 2, 2:3]).then_inc(sem["pe"], 1)

            def att_t(i):
                act.wait_ge(sem["at"], i + 1)
                if i >= 2:
                    act.wait_ge(sem["ao"], i - 1)
                if i % 2 == 0:
                    act.activation(att_p[0][:, 0:3], quad(4)[:, 0:3], ACT.Copy).then_inc(sem["pt"], 1)
                else:
                    act.activation(att_p[1][:, 0:4], quad(4), ACT.Copy)
                    act.activation(att_p[1][:, 4:6], quad(5)[:, 0:2], ACT.Copy).then_inc(sem["pt"], 1)

            def att_o(i):
                act.wait_ge(sem["ao"], i + 1)
                high(Oh[:, i // 2, i % 2 * P:(i % 2 + 1) * P], quad(1)[:, 0], 1.0, "oah")

            def ret_o(i):
                act.wait_ge(sem["bag"], i + 1)
                act.activation(rsd[:, i % 2, 0:1], bag[:, i % 2, 1:2], ACT.Ln, bias=pcol("eps")).then_inc(sem["rl"], 1)
                act.wait_ge(sem["rl"], i + 1)
                act.activation(rsd[:, i % 2, 1:2], rsd[:, i % 2, 0:1], ACT.Exp, scale=-0.5).then_inc(sem["rr"], 1)

            def ret_t(i):
                h, t = i // 2, i % 2
                act.wait_ge(sem["rtT"], i + 1)
                act.wait_ge(sem["or"], i - 1) if i >= 2 else act.wait_ge(sem["qk"], 24)
                tt = t2[i % 2][:].rearrange("p a (c m) -> p (a c) m", m=P)
                for f in range(4):
                    a = act.activation(tt[:, f], quad(i % 2)[:, f], ACT.Identity, scale=pcol("gn_g", 4 * h + f),
                                       bias=pcol("gn_b", 4 * h + f))
                a.then_inc(sem["rt"], 1)
                act.wait_ge(sem["rg"], i + 1)
                dst = (Zh, Xh)[h // 2][:, 4 * (h % 2):4 * (h % 2) + 4, t * P:(t + 1) * P]
                high(dst, tt, 1.0, "orh")

            def mix2(j):
                act.wait_ge(sem["m20"], j + 1)
                high(pair(Yh, j), t2[j % 2][:], 1.0, "m2h")

            def ffn2(j):
                act.wait_ge(sem["ev"], GRP[("u2", j)] + 1)
                act.activation(pair((Yh, Zh)[j // 4 % 2], j % 4), y[j % 2][:], ACT.Square).then_inc(sem["f2h"], 1)

            steps = {"x0": x0, "norm": norm, "conv4": conv4, "gatec": gatec, "conv3": conv3, "silu": silu, "sig": sig,
                     "zg": zg, "silur": silur, "ffn1": ffn1, "l2n": l2n, "ab_mm": ab_mm, "ab_cum": ab_cum,
                     "rows": rows, "mixc": mixc, "lev0t": lev0t, "level": level, "uw": uw, "state": state, "o": o,
                     "onorm": onorm, "mix": mix, "res1": res1, "res2": res2, "res3": res3, "sqh": sqh, "rmsh": rmsh,
                     "att_s": att_s_, "att_t": att_t, "att_o": att_o, "ret_o": ret_o, "ret_t": ret_t, "mix2": mix2,
                     "ffn2": ffn2}
            for n in range(-1, NB):
                if n == -1:
                    x0()
                    for m in range(3):
                        split(m)
                        if m == 0:
                            act.wait_ge(sem["abw"], 16)
                            act.activation(abh[:], abw, ACT.Copy).then_inc(sem["abh"], 1)
                    continue
                if n + 3 < NB:
                    split(n + 3)
                for step, a in TODO[n]:
                    if step in steps:
                        steps[step](*a)

        @block.vector
        def _(dve):
            def tt(out, a, b, op, name):
                dve.tensor_tensor(out, a, b, op).then_inc(sem[name], 1)

            def stt(out, a, s, b, op0, op1, name):
                dve.scalar_tensor_tensor(out=out, in0=a, scalar=s, in1=b, op0=op0, op1=op1).then_inc(sem[name], 1)

            def split(n):
                dve.wait_ge(sem["wh"], n + 1)
                tt(wl[:, n % 3], raw[:, n % 2], f32(wh[:, n % 3]), ALU.subtract, "wl")

            def low(dst, src, hi, name_hi, v, name):
                dve.wait_ge(sem[name_hi], v)
                tt(dst, src, f32(hi), ALU.subtract, name)

            def take(n):
                key = kind, j = SEQ[n]
                if key not in RING:
                    return
                dve.wait_ge(sem["mm"], n + 1)
                ps = ring(key)[:]
                if kind in YKINDS:
                    if key == ("k", 0):
                        dve.wait_ge(sem["rb"], 1)
                    if kind == "u1" and j == 0:
                        dve.wait_ge(sem["rb"], 2)
                    before = SEQ[n - 2] if n >= 2 else None
                    if before in SIG:
                        dve.wait_ge(sem["sg"], SIG[before] + 1)
                    if before and before[0] in ("z", "gr"):
                        dve.wait_ge(sem["zs" if before[0] == "z" else "sr"], before[1] + 1)
                    tt(y[n % 2][:], ps, two(rb[:]), ALU.mult, "ev")
                elif kind == "c":
                    if j:
                        dve.wait_ge(sem["cx"], j)
                    tt(cg[:], ps, two(rb[:]), ALU.mult, "ev")
                elif kind == "b":
                    if j:
                        dve.wait_ge(sem["mc"], j)
                    tt(bg[:], ps, two(rb[:]), ALU.mult, "ev")
                elif kind == "wa":
                    dve.wait_ge(sem["sg"], SIG[("ga", j)] + 1)
                    tt(pair(m1, j), ps, e[j % 2][:], ALU.mult, "ev")
                elif kind == "wb":
                    dve.wait_ge(sem["sg"], SIG[("gb", j)] + 1)
                    tt(t2[j % 2][:], ps, pair(sgb, j), ALU.mult, "ev")
                elif kind == "wo":
                    dve.wait_ge(sem["xres"], 16)
                    dve.wait_ge(sem["mx0"], 4)
                    tt(pair(xT, j), ps, pair(xres, j), ALU.add, "ev")
                elif kind in ("qa", "ka", "qr", "kr"):
                    if kind == "qa" and j == 0:
                        dve.wait_ge(sem["rb"], 3)
                    tt(pair({"qa": qa, "ka": ka, "qr": qr, "kr": kr}[kind], j), ps, two(rb[:]), ALU.mult, "ev")
                elif kind in ("va", "vr"):
                    if kind == "va" and j == 0:
                        dve.wait_ge(sem["rtk"], 1)
                    if kind == "vr" and j == 0:
                        dve.wait_ge(sem["as"], 8)
                    tt((va if kind == "va" else vr)[:, :, j * S:(j + 1) * S], ps,
                       rtok[:].unsqueeze(2).broadcast_to([P, 2, S]), ALU.mult, "ev")
                elif kind == "pb":
                    dve.wait_ge(sem["sg"], SIG[("tb", j // 2)] + 1)
                    if j < 4:
                        dve.wait_ge(sem["or"], 8)
                    tt(t2[j // 2 % 2][:], ps, tb(j // 2), ALU.mult, "ev")
                elif kind == "w2":
                    tt(pair(xT, j), ps, pair(xT, j), ALU.add, "ev")
                elif kind == "u2":
                    if j == 0:
                        dve.wait_ge(sem["rb"], 4)
                    if j >= 2:
                        dve.wait_ge(sem["fq2"], j - 1)
                    stt(y[j % 2][:], ps, 0.0, two(rb[:]), ALU.max, ALU.mult, "ev")

            def x0():
                dve.memset(G2[:], 0.0).then_inc(sem["g2z"], 1)
                dve.wait_ge(sem["par"], 16)
                dve.wait_ge(sem["xT"], 16)
                tt(gg, par[:, PAR["g_fin"]:PAR["g_fin"] + 8], par[:, PAR["g_n1"]:PAR["g_n1"] + 8], ALU.mult, "gg")
                for k in range(KT):
                    dve.wait_ge(sem["x0h"], k + 1)
                    stt(Xl[:, k], xT[:, k], pcol("g_mix", k), f32(Xh[:, k]), ALU.mult, ALU.subtract, "x0")

            def norm(i):
                if i != 2:
                    return
                dve.wait_ge(sem["nl"], 4)
                tt(lnt[:], psA[5][:, 1], rfin[:], ALU.mult, "ms0")
                dve.wait_ge(sem["ms0"], 1)
                tt(lnt[:], lnt[:], rfin[:], ALU.mult, "ms")
                dve.wait_ge(sem["nl"], 6)
                tt(rb[:], lnt[:], rfin[:], ALU.mult, "rb")

            def conv(a, cols, taps):
                i = CONV[a]
                dve.wait_ge(sem["tap"], i + 1)
                first = TAPS[a] - 2 * (taps - 1)
                for d in range(1, taps):
                    for f in range(2):
                        if d > 1:
                            dve.wait_ge(sem["cv"], first + 2 * (d - 2) + f + 1)
                        stt(acc[i % 2][:, f, d:S], yk(a)[:, f, 0:S - d], cols(taps - 1 - d, f), acc[i % 2][:, f, d:S],
                            ALU.mult, ALU.add, "cv")

            def conv4(kind, j):
                c = {"q": 0, "k": 8, "v": 16}[kind] + 2 * j
                conv((kind, j), lambda tap, f: pcol("conv_g", 24 * tap + c + f), 4)

            def gatec(j):
                conv(("x", j), lambda tap, f: pcol("conv_a", 8 * tap + 2 * j + f), 3)

            def conv3(j):
                conv(("u1", j), lambda tap, f: pcol("conv_f", 2 * FF1 * tap + j + f * FF1), 3)

            def zg(j):
                low(pair(Yl, j), t2[j % 2][:], pair(Yh, j), "ogh", j + 1, "og")

            def ffn1(j):
                h, l = ((Xh, Xl), (Zh, Zl), (Xh, Xl))[j // 8]
                low(l[:, j % 8], t2[j % 2][:, 1], h[:, j % 8], "f1h", j + 1, "f1")

            def ab_mm():
                n = [0]

                def then(ins):
                    n[0] += 1
                    ins.then_inc(sem["abv"], 1)
                    dve.wait_ge(sem["abv"], n[0])

                dve.wait_ge(sem["ab"], 1)
                dve.wait_ge(sem["g2z"], 1)
                then(dve.tensor_tensor(abt[:, 0], psA[4][0:64, 0], rb[0:64], ALU.mult))
                u, m = abt[0:8, 1], abt[0:8, 2]
                then(dve.tensor_scalar(u, abt[0:8, 0], pcol("dt_b", hi=8), None, ALU.add))
                then(dve.scalar_tensor_tensor(out=m, in0=u, scalar=-1.0, in1=u, op0=ALU.mult, op1=ALU.max))
                dve.wait_ge(sem["aba"], 3)
                x, s = abt[0:8, 0], G3
                then(dve.tensor_scalar(s, x, 1.0, None, ALU.add))
                g = G2[0:8]
                then(dve.scalar_tensor_tensor(out=g, in0=s, scalar=-1.0, in1=x, op0=ALU.add, op1=ALU.subtract))
                dve.wait_ge(sem["aba"], 4)
                then(dve.reciprocal(s, s))
                then(dve.tensor_tensor(g, g, s, ALU.mult))
                then(dve.tensor_tensor(g, m, g, ALU.subtract))
                then(dve.scalar_tensor_tensor(out=g, in0=u, scalar=0.0, in1=g, op0=ALU.max, op1=ALU.add))
                dve.tensor_scalar(g, g, small[0:8, 8:9], -1.0, ALU.mult, ALU.mult).then_inc(sem["g2"], 1)
                b = abt[32:40, 1]
                then(dve.tensor_scalar(b, b, 1.0, None, ALU.add))
                dve.reciprocal(G2[32:40], b).then_inc(sem["g2"], 1)

            def ab_tok():
                dve.wait_ge(sem["abT"], 1)
                dve.tensor_copy(gtok[:], flat(4)[:, 0:80].rearrange("p (t c) -> p t c", t=2)).then_inc(sem["gtok"], 1)

            def ab_cum():
                dve.wait_ge(sem["cum"], 1)
                dve.tensor_copy(Gs[:], flat(4)[:, 0:64]).then_inc(sem["gs"], 1)
                dve.tensor_copy(G3, psA[4][0:8, 1]).then_inc(sem["g3"], 1)
                dve.wait_ge(sem["gs"], 1)
                ht = "p (t h) -> p h t"
                dve.tensor_scalar(TS[:, 0], Gs[:, 0:16].rearrange(ht, t=2), -1.0, None, ALU.mult).then_inc(sem["gs"], 1)
                tt(TS[:, 3], Gs[:, 16:32].rearrange(ht, t=2), Gs[:, 0:16].rearrange(ht, t=2), ALU.subtract, "gs")
                dve.tensor_copy(TS[:, 1], gtok[:, :, 32:40].rearrange("p t h -> p h t")).then_inc(sem["tb"], 1)
                dve.wait_ge(sem["tb"], 1)
                dve.wait_ge(sem["tsa"], 1)
                tt(TS[:, 2], TS[:, 1], TS[:, 4], ALU.mult, "tb")

            def rows(h):
                dve.wait_ge(sem["row"], h + 1)
                dve.wait_ge(sem["kn"], 8)
                tt(kb[:, h], kn[:, h], psA[4 * (h % 2)][:, 0], ALU.mult, "kb")
                tt(DT[:, h].rearrange("p (t m) -> p t m", t=2), psA[4 * (h % 2) + 1][:, 1].rearrange("p (t m) -> p t m", t=2),
                   negm.unsqueeze(1).broadcast_to([P, 2, P]), ALU.add, "kb")

            def kk(h):
                dve.wait_ge(sem["kk"], h + 1)
                dve.wait_ge(sem["dt"], h + 1)
                v = psA[2 + h % 2][:].rearrange("p t (w m) -> p t w m", w=2)
                d = DT[:, h].rearrange("p (t m) -> p t m", t=2)
                tt(LT[:, h].rearrange("p (t m) -> p t m", t=2), v[:, :, 0], d, ALU.mult, "lt")
                tt(AQ[:, h].rearrange("p (t m) -> p t m", t=2), v[:, :, 1], d, ALU.mult, "lt")

            def tok(b):
                def col(i):
                    return TS[:, i, 2 * b:2 * b + 2].unsqueeze(3).broadcast_to([P, 2, 2, P])

                dve.wait_ge(sem["tk"], 2 * b + 1)
                if b == 0:
                    dve.wait_ge(sem["tb"], 2)
                    dve.wait_ge(sem["tsa"], 3)
                v = psA[4][:].rearrange("p a (c m) -> p a c m", m=P)
                tt(KBE[:, 2 * b:2 * b + 2], v, col(2), ALU.mult, "tok")
                tt(KD[:, 2 * b:2 * b + 2], v, col(3), ALU.mult, "tok")
                dve.wait_ge(sem["tk"], 2 * b + 2)
                v = psA[5][:].rearrange("p a (c m) -> p a c m", m=P)
                tt(VB[:, 2 * b:2 * b + 2], v, col(1), ALU.mult, "tok")

            def level(l):
                for b in range(4):
                    i = 4 * l + b
                    dve.wait_ge(sem["pb_"], i + 1)
                    for q, dst in enumerate((SI, TI)[:2 if l < 4 else 1]):
                        v = dst[:, 2 * b:2 * b + 2]
                        tt(v, v, psA[2 * (b % 2) + q][:].rearrange("p a (c m) -> p a c m", m=P), ALU.subtract, "st")

            def state(c):
                if c:
                    dve.wait_ge(sem["sp"], c + 1)
                    dve.wait_ge(sem["dec"], c)
                    for q in range(2):
                        tt(hist[c][:, 4 * q:4 * q + 4], dec[:, 4 * q:4 * q + 4], quad(4 + q), ALU.add, "h")

            def wstate(c):
                t, r = c // 2, slice(CHUNK * (c % 2), CHUNK * (c % 2) + CHUNK)
                dve.wait_ge(sem["ws"], c)
                for q in range(2):
                    v = U[r, 4 * q:4 * q + 4, t]
                    tt(v, v, psA[q][r].rearrange("p a (c m) -> p (a c) m", m=P), ALU.subtract, "vn")

            def onorm(q):
                dve.wait_ge(sem["ri"], HEADN[(q,)] + 1)
                v = pair(OT, q)
                stt(v, v, pcol("g_o"), t2[q % 2][:], ALU.mult, ALU.mult, "on")

            def mixc(j):
                low(pair(Yl, j), t2[j % 2][:], pair(Yh, j), "yah", j + 1, "ya")

            def mix(j):
                low(pair(Xl, j), t2[j % 2][:], pair(Xh, j), "mxh", j + 1, "mx")

            def gained(dst, hi, gain, name_hi, name, j):
                for k in (2 * j, 2 * j + 1):
                    dve.wait_ge(sem[name_hi], k + 1)
                    stt(dst[:, k], xT[:, k], gain(k), f32(hi[:, k]), ALU.mult, ALU.subtract, name)

            def res1(j):
                gained(Yl, Yh, lambda k: pcol("g_ffn", k), "x1h", "x1", j)

            def res2(j):
                dve.wait_ge(sem["mm"], AT[("d1", (8, 9, 10, 10)[j])] + 1)
                tt(pair(xT, j), psA[j][:], pair(xT, j), ALU.add, "r2")
                gained(Yl, Yh, lambda k: gg[:, k:k + 1], "xbh", "xb", j)

            def res3(j):
                gained(Xl, Xh, lambda k: pcol("g_n2", k), "x3h", "x3", j)

            def x2():
                for k in range(KT):
                    stt(xT[:, k], xT[:, k], pcol("g_fin", k), rfin[:], ALU.mult, ALU.mult, "x2")

            def rtok_():
                dve.wait_ge(sem["rtp"], 1)
                dve.tensor_copy(rtok[:], flat(4)[:, 0:2]).then_inc(sem["rtk"], 1)

            def rmsh(kind, j):
                i = HEADN[(kind, j)]
                dve.wait_ge(sem["ri"], i + 1)
                for f in range(2):
                    v = QK[kind][:, 2 * j + f]
                    stt(v, v, pcol("g_q" if kind == "qa" else "g_k", 2 * j + f), t2[i % 2][:, f], ALU.mult, ALU.mult, "qk")

            def att_s_(i):
                hp, t = i // 2, i % 2
                n = P * (t + 1)
                dve.wait_ge(sem["as"], i + 1)
                if i == 0:
                    dve.wait_ge(sem["md"], 16)
                if i >= 2:
                    dve.wait_ge(sem["at"], i - 1)
                buf = att_s[i % 2].rearrange("p a b -> p (a b)")
                for g in range(3):
                    slope = float(np.float32(2.0 ** (-8.0 * (4 * g + hp + 1) / HA)))
                    src = flat(0)[:, g * P:(g + 1) * P] if t == 0 else psA[2 + g // 2][:, g % 2]
                    stt(buf[:, g * n:(g + 1) * n], md[:, g, S - n:S], -slope / SCALE, src, ALU.mult, ALU.add, "sc")
                dve.wait_ge(sem["sc"], 3 * i + 3)
                dve.tensor_reduce(atn[:, t, 0:1], buf[:, 0:3 * n], AX.X, ALU.max).then_inc(sem["am"], 1)
                dve.wait_ge(sem["am"], i + 1)
                dve.tensor_scalar(atn[:, t, 1:2], atn[:, t, 0:1], -SCALE, None, ALU.mult).then_inc(sem["nm"], 1)
                dve.wait_ge(sem["pe"], i + 1)
                dve.reciprocal(atn[:, t, 3:4], atn[:, t, 2:3]).then_inc(sem["rd"], 1)
                dve.wait_ge(sem["rd"], i + 1)
                dve.tensor_scalar(buf[:, 0:3 * n], buf[:, 0:3 * n], atn[:, t, 3:4], None, ALU.mult).then_inc(sem["pn"], 1)

            def att_o(i):
                s = slice(i % 2 * P, (i % 2 + 1) * P)
                low(Ol[:, i // 2, s], quad(1)[:, 0], Oh[:, i // 2, s], "oah", i + 1, "oa")

            def ret_s(h):
                dve.wait_ge(sem["rsp"], h + 1)
                if h == 0:
                    dve.wait_ge(sem["dr"], 16)
                b = 2 * (h % 2)
                tt(ST[h][:, 0:S], psA[b][:, 0], dr[:, h], ALU.mult, "rs")
                tt(ST[h][:, S:S + P], psA[b][:, 1, 0:P], dr[:, h, 0:P], ALU.mult, "rs")

            def ret_o(i):
                dve.wait_ge(sem["ro"], i + 1)
                dve.bn_stats(bst[:, i % 2], flat(4 + i % 2)).then_inc(sem["bst"], 1)
                dve.wait_ge(sem["bst"], i + 1)
                dve.bn_aggr(bag[:, i % 2], bst[:, i % 2]).then_inc(sem["bag"], 1)
                dve.wait_ge(sem["rr"], i + 1)
                if i >= 2:
                    dve.wait_ge(sem["rtT"], i - 1)
                dve.tensor_scalar(acc[i % 2][:], psA[4 + i % 2][:], bag[:, i % 2, 0:1], rsd[:, i % 2, 1:2],
                                  ALU.subtract, ALU.mult).then_inc(sem["ry"], 1)

            def ret_t(i):
                h, t = i // 2, i % 2
                s = (slice(None), slice(4 * (h % 2), 4 * (h % 2) + 4), slice(t * P, (t + 1) * P))
                low((Zl, Xl)[h // 2][s], t2[i % 2][:].rearrange("p a (c m) -> p (a c) m", m=P), (Zh, Xh)[h // 2][s],
                    "orh", i + 1, "or")

            def ma():
                dve.wait_ge(sem["mm"], AT[("pa", 1)] + 1)
                dve.wait_ge(sem["sg"], SIG[("ta", 3)] + 1)
                for q in range(4):
                    tt(pair(ta, q), psA[q][:], pair(ta, q), ALU.mult, "ma")

            def mix2(j):
                low(pair(Yl, j), t2[j % 2][:], pair(Yh, j), "m2h", j + 1, "m2")

            def ffn2(j):
                dve.wait_ge(sem["fq2"], j + 1)
                h, l = ((Yh, Yl), (Zh, Zl))[j // 4 % 2]
                low(pair(l, j % 4), t2[j % 2][:], pair(h, j % 4), "f2h", j + 1, "f2")

            def res4(q):
                dve.wait_ge(sem["mm"], AT[("d2", 12 + q)] + 1)
                tt(pair(xT, q), psA[q][:], pair(xT, q), ALU.add, "res4")

            steps = {"norm": norm, "conv4": conv4, "gatec": gatec, "conv3": conv3, 
                     "zg": zg, "ffn1": ffn1, "ab_mm": ab_mm, "ab_tok": ab_tok, "ab_cum": ab_cum,
                     "rows": rows, "kk": kk, "tok": tok, "level": level, "state": state, "wstate": wstate,
                     "onorm": onorm, "mixc": mixc, "mix": mix, "res1": res1, "res2": res2, "res3": res3, "x2": x2,
                     "rtok": rtok_, "rmsh": rmsh, "att_s": att_s_, "att_o": att_o, "ret_s": ret_s, "ret_o": ret_o,
                     "ret_t": ret_t, "ma": ma, "mix2": mix2, "ffn2": ffn2, "res4": res4}
            for n in range(-1, NB):
                if n == -1:
                    x0()
                    for m in range(3):
                        split(m)
                        if m == 0:
                            dve.wait_ge(sem["abh"], 1)
                            tt(abl[:], abw, f32(abh[:]), ALU.subtract, "abl")
                    continue
                take(n)
                if n + 3 < NB:
                    split(n + 3)
                for step, a in TODO[n]:
                    if step in steps:
                        steps[step](*a)

        @block.gpsimd
        def _(pool):
            def tt(out, a, b, op, name):
                pool.tensor_tensor(out, a, b, op).then_inc(sem[name], 1)

            def x0():
                pool.wait_ge(sem["xT"], 16)
                for j in range(4):
                    if j >= 2:
                        pool.wait_ge(sem["ss0"], j - 1)
                    tt(sq[j % 2][:] if j else ss[0][:], pair(xT, j), pair(xT, j), ALU.mult, "sq0")
                    pool.wait_ge(sem["sq0"], j + 1)
                    if j:
                        if j > 1:
                            pool.wait_ge(sem["ss0"], j - 1)
                        tt(ss[0][:], ss[0][:], sq[j % 2][:], ALU.add, "ss0" if j < 3 else "ss")

            def silu(kind, j):
                if kind != "v":
                    m = HEADN[(kind, j)]
                    pool.wait_ge(sem["silu"], SILU[(kind, j)] + 1)
                    if m >= 2:
                        pool.wait_ge(sem["hsum"], m - 1)
                    else:
                        pool.wait_ge(sem["ss"], 1)
                    dst = pair(QKV[kind], j)
                    tt(sq[m % 2][:], dst, dst, ALU.mult, "sq")

            def l2n(kind, j):
                pool.wait_ge(sem["ri"], HEADN[(kind, j)] + 1)
                v = pair(QKV[kind], j)
                tt(v, v, t2[HEADN[(kind, j)] % 2][:], ALU.mult, "kn")

            def gatec(j):
                pool.wait_ge(sem["ev"], GRP[("x", j)] + 1)
                v = y[AT[("x", j)] % 2][:]
                tt(v, v, cg[:], ALU.mult, "cx")

            def mixc(j):
                pool.wait_ge(sem["cv"], TAPS[("x", j)])
                pool.wait_ge(sem["ev"], GRP[("b", j)] + 1)
                pool.wait_ge(sem["ya"], j - 1) if j >= 2 else pool.wait_ge(sem["qd"], 8)
                tt(t2[j % 2][:], acc[CONV[("x", j)] % 2][:], bg[:], ALU.mult, "mc")

            def rows(h):
                pool.wait_ge(sem["eg"], h + 1)
                if h == 0:
                    pool.wait_ge(sem["kn"], 8)
                tt(qd[:, h], qn[:, h], t2[h % 2][:, 0], ALU.mult, "qd")

            def lev0():
                pool.wait_ge(sem["mask"], 16)
                pool.wait_ge(sem["kk"], 8)
                for b in range(4):
                    pool.wait_ge(sem["lt"], 4 * b + 4)
                    if b >= 2:
                        pool.wait_ge(sem["s0"], 2 * b - 2)
                    v = LT[:, 2 * b:2 * b + 2].rearrange("p h (t m) -> p (h t) m", m=P)
                    s = sq[b % 2][:].rearrange("p a (c m) -> p (a c) m", m=P)
                    tt(s, v, mask[:, 0].unsqueeze(1).broadcast_to([P, 4, P]), ALU.mult, "s0")
                    pool.wait_ge(sem["s0"], 2 * b + 1)
                    tt(SI[:, 2 * b:2 * b + 2].rearrange("p h t m -> p (h t) m"),
                       ident.unsqueeze(1).broadcast_to([P, 4, P]), s, ALU.subtract, "s0")

            def level(l):
                for b in range(4):
                    i = 4 * l + b
                    if i >= 2:
                        pool.wait_ge(sem["pa_"], i - 1)
                    else:
                        pool.wait_ge(sem["s0"], 8)
                    v = LT[:, 2 * b:2 * b + 2].rearrange("p h (t m) -> p (h t) m", m=P)
                    tt(sq[b % 2][:].rearrange("p a (c m) -> p (a c) m", m=P), v,
                       mask[:, l + 1].unsqueeze(1).broadcast_to([P, 4, P]), ALU.mult, "bs")

            def state(c):
                if c == 2:
                    return
                pool.wait_ge(sem["h0"], 2) if c == 0 else pool.wait_ge(sem["h"], 2)
                tt(dec, hist[c], egl[:, c + 1].unsqueeze(2).broadcast_to([P, H1, P]), ALU.mult, "dec")

            def osq(q):
                m = HEADN[(q,)]
                pool.wait_ge(sem["oc"], 4)
                pool.wait_ge(sem["hsum"], m - 1)
                if q < 2:
                    pool.wait_ge(sem["pa_"], 20)
                tt(sq[m % 2][:], pair(OT, q), pair(OT, q), ALU.mult, "sq")

            def zg(j):
                pool.wait_ge(sem["zs"], j + 1)
                pool.wait_ge(sem["on"], 4)
                if j >= 2:
                    pool.wait_ge(sem["og"], j - 1)
                tt(t2[j % 2][:], e[j % 2][:], pair(OT, j), ALU.mult, "zp")

            def mix(j):
                pool.wait_ge(sem["ev"], GRP[("wb", j)] + 1)
                tt(t2[j % 2][:], t2[j % 2][:], pair(m1, j), ALU.add, "mx0")

            def add_squares(i, j):
                base = {1: 0, 2: 3, 3: 10}[i]
                per = 2 if i == 2 else 1
                done = {1: 0, 2: 4, 3: 12}[i]
                for g in range(per):
                    pool.wait_ge(sem["sqr"], done + per * j + g + 1)
                    src = (sq, t2)[g][j % 2][:]
                    last = j == 3 and g == per - 1
                    name = "ss" if last else "ssa"
                    if j == 0:
                        if i > 1 or g == 0:
                            pool.wait_ge(sem["nsum"], i)
                        pool.tensor_copy(ss[g][:], src).then_inc(sem[name], 1)
                    else:
                        pool.wait_ge(sem["ssa"], base + per * (j - 1) + g + 1)
                        tt(ss[g][:], ss[g][:], src, ALU.add, name)

            def ffn1(j):
                pool.wait_ge(sem["fs"], j + 1)
                pool.wait_ge(sem["f1"], j - 1) if j >= 2 else pool.wait_ge(sem["mx"], 4)
                tt(t2[j % 2][:, 1], e[j % 2][:, 0], acc[CONV[("u1", j)] % 2][:, 1], ALU.mult, "fp")

            def ret_t(i):
                h, t = i // 2, i % 2
                pool.wait_ge(sem["rt"], i + 1)
                pool.wait_ge(sem["sr"], 2 * h + 2)
                v = t2[i % 2][:].rearrange("p a (c m) -> p (a c) m", m=P)
                tt(v, v, gr[:, 4 * h:4 * h + 4, t * P:(t + 1) * P], ALU.mult, "rg")

            def mix2(j):
                pool.wait_ge(sem["ev"], GRP[("pb", 2 * j)] + 1)
                pool.wait_ge(sem["ma"], 4)
                tt(t2[j % 2][:], t2[j % 2][:], pair(ta, j), ALU.add, "m20")

            def ffn2(j):
                pool.wait_ge(sem["ev"], GRP[("u2", j)] + 1)
                pool.wait_ge(sem["f2"], j - 1) if j >= 2 else pool.wait_ge(sem["m2"], 4)
                tt(t2[j % 2][:], y[j % 2][:], y[j % 2][:], ALU.mult, "fq2")

            steps = {"x0": x0, "silu": silu, "l2n": l2n, "gatec": gatec, "mixc": mixc, "rows": rows,
                     "lev0": lev0, "level": level, "state": state, "osq": osq, "zg": zg, "mix": mix,
                     "res1": lambda j: add_squares(1, j), "res2": lambda j: add_squares(2, j),
                     "res3": lambda j: add_squares(3, j), "ffn1": ffn1, "ret_t": ret_t,
                     "mix2": mix2, "ffn2": ffn2}
            for n in range(-1, NB):
                for step, a in TODO[n]:
                    if step in steps:
                        steps[step](*a)


def blocks(matrix, name):
    w = matrix.reshape(matrix.shape[0] // P, P, matrix.shape[1] // P, P)
    at = [(n, pairs(*key)[1]) for n, key in enumerate(SEQ) if pairs(*key)[0] == name]
    k = np.array([[a for a, _ in prs] for _, prs in at])
    c = np.array([[b for _, b in prs] for _, prs in at])
    return [n for n, _ in at], w[k, :, c, :].transpose(0, 2, 1, 3)


def channels(a):
    return a.reshape(-1, P).T


def delta_constants():
    j, i = np.arange(P)[:, None], np.arange(P)[None, :]
    same = j // CHUNK == i // CHUNK
    sums = [np.where(same & (i >= j), 0.0, NEG)]
    cols = []
    for s in (1, 2, 4, 8, 16, 32):
        cols.append((j // (2 * s) == i // (2 * s)) & (i % (2 * s) >= s) & (j % (2 * s) < s))
    sums += [same & (j <= i), same, (j < CHUNK) & (i >= 0), (j >= CHUNK) & (i >= 0)]
    return [np.stack([c.astype(np.float32) for c in v], axis=1) for v in (sums, cols)]


def attention_constants():
    i, j = np.arange(P)[:, None] + P, np.arange(S)[None, :]
    d = i - j
    return np.concatenate([np.where((d >= 0) & (d % dil == 0) & (d <= reach), d, BIG).astype(np.float32)
                           for dil, reach in ((1, 128), (4, 512), (16, 2048))], axis=1)


def retention_constants():
    j, i = np.arange(P)[:, None], np.arange(S)[None, :]
    cols = []
    for h in range(RH):
        log_g = np.log(1.0 - 2.0 ** (-5.0 - h))
        cols.append(np.where(i >= j, np.exp(log_g * np.maximum(i - j, 0)) * 256.0 ** -0.5, 0.0).astype(np.float32))
    return np.concatenate(cols, axis=1)


def kernel(**inputs):
    import concourse.bacc as bacc
    from concourse.bass_utils import run_bass_kernel_spmd

    a = {name: np.asarray(v) for name, v in inputs.items()}
    w_in = a["w_in"][0]
    wts = np.empty((NB, P, 16, P), np.float32)
    for name, m in (("w_in", w_in[:, :7168]), ("w_gates", w_in[:, 7184:]), ("w_a_out", a["w_a_out"][0]),
                    ("w_b_out", a["w_b_out"][0]), ("w_o", a["w_o"][0]), ("w_up", a["w_up"][0]),
                    ("w_down", a["w_down"][0]), ("w_in_2", a["w_in_2"][0]), ("w_proj_a_2", a["w_proj_a_2"][0]),
                    ("w_proj_b_2", a["w_proj_b_2"][0]), ("w_out_2", a["w_out_2"][0]), ("w_up_2", a["w_up_2"][0]),
                    ("w_down_2", a["w_down_2"][0])):
        at, b = blocks(m, name)
        wts[at] = b
    par = np.zeros((P, NPAR), np.float32)
    for name, v in (("g_mix", "norm_mix_g"), ("conv_a", "conv_a_w"), ("conv_g", "gdn_conv_w"), ("g_ffn", "norm_ffn_g"),
                    ("conv_f", "ffn_conv_w"), ("g_fin", "norm_final_g"), ("g_n1", "norm1_g_2"), ("g_q", "q_norm_g_2"),
                    ("g_k", "k_norm_g_2"), ("gn_g", "ret_gn_g_2"), ("gn_b", "ret_gn_b_2"), ("g_n2", "norm2_g_2"),
                    ("g_o", "gdn_norm_g")):
        v = channels(a[v])
        par[:, PAR[name]:PAR[name] + v.shape[1]] = v
    par[0:8, PAR["a_log"]] = a["gdn_A_log"][0]
    par[0:8, PAR["dt_b"]] = a["gdn_dt_bias"][0]
    par[:, PAR["eps"]] = EPS
    par[:, PAR["one"]] = 1.0
    par[:, PAR["ln_scale"]] = np.log(SCALE)
    par[:, PAR["ident"]:PAR["ident"] + P] = np.eye(P)
    par[:, PAR["ones"]:PAR["ones"] + P] = 1.0
    abw = np.zeros((P, KT, 64), np.float32)
    ab = w_in[:, 7168:7184].reshape(KT, P, 16).transpose(1, 0, 2)
    abw[:, :, 0:8], abw[:, :, 32:40] = ab[:, :, 0:8], ab[:, :, 8:16]
    sel = np.zeros((P, H1, P), np.float32)
    for h in range(H1):
        sel[h, h], sel[32 + h, h] = 1.0, 1.0
    sums, masks = delta_constants()
    x = a["x"][0].reshape(S, KT, P).transpose(2, 1, 0)
    arrays = {"wts": wts, "par": par, "x": x, "abw": abw, "sums": sums, "mask": masks, "sel": sel,
              "md": attention_constants(), "dr": retention_constants()}
    nc = bacc.Bacc("TRN2", target_bir_lowering=False, num_devices=1)
    args = []
    for name, v in arrays.items():
        arrays[name] = np.ascontiguousarray(v)
        args.append(nc.dram_tensor("in_" + name, v.shape, F32, kind="ExternalInput").ap())
    args.append(nc.dram_tensor("out", (P, KT, S), F32, kind="ExternalOutput").ap())
    program(nc, *args)
    r = run_bass_kernel_spmd(nc, [{"in_" + name: v for name, v in arrays.items()}], core_ids=[0])
    out = r.results[0]["out"]
    return out.transpose(2, 1, 0).reshape(1, S, D)
```

```python
from contextlib import ExitStack

import numpy as np

import concourse.bass as bass
from concourse import mybir

ALU = mybir.AluOpType
ACT = mybir.ActivationFunctionType
AX = mybir.AxisListType
F32 = mybir.dt.float32
F32R = mybir.dt.float32r

P = 128
D = 1024
S = 256
KT = D // P
EPS = 1e-6
H1 = 8
FF1 = 2816 // P
HA, HG = 12, 4
RH = 4
BIG = 1e30
NEG = -1e30
SCALE = float(P) ** -0.5


def plan():
    seq = [(kind, j) for kind in "kqv" for j in range(4)]
    seq += [(kind, j) for j in range(4) for kind in ("c", "x", "b")]
    seq += [(kind, j) for j in range(4) for kind in ("ga", "wa")]
    seq += [("gb", j) for j in range(3)] + [("z", j) for j in range(4)] + [("gb", 3)]
    seq += [("wb", j) for j in range(4)] + [("wo", j) for j in range(4)]
    seq += [("u1", j) for j in range(10)] + [("d1", j) for j in range(4)]
    seq += [("u1", j) for j in range(10, FF1)] + [("d1", j) for j in range(4, 11)]
    seq += [("qa", j) for j in range(6)] + [("ka", j) for j in range(6)] + [("va", j) for j in range(6)]
    seq += [("kr", j) for j in range(4)] + [("qr", j) for j in range(4)]
    seq += [("vr", j) for j in range(8)] + [("gr", j) for j in range(8)]
    seq += [("ta", j) for j in range(4)] + [("tb", j) for j in range(4)]
    seq += [("pa", j) for j in range(2)] + [("pb", j) for j in range(8)] + [("w2", j) for j in range(4)]
    seq += [("u2", j) for j in range(8)]
    for g in range(1, 4):
        seq += [("d2", 4 * (g - 1) + j) for j in range(4)]
        if g < 3:
            seq += [("u2", 4 * (g + 1) + j) for j in range(4)]
    seq += [("d2", 12 + j) for j in range(4)]
    return seq


SEQ = plan()
NB = len(SEQ)
AT = {key: n for n, key in enumerate(SEQ)}
COL1 = {"b": 0, "c": 8, "x": 16, "q": 24, "k": 32, "v": 40, "z": 48}
COL2 = {"qa": 0, "ka": 12, "va": 24, "qr": 36, "kr": 44, "vr": 52, "gr": 68, "ta": 84, "tb": 92}


def pairs(kind, j):
    two = [(k, c) for k in range(KT) for c in (2 * j, 2 * j + 1)]
    if kind in COL1:
        return "w_in", [(k, COL1[kind] + c) for k, c in two]
    if kind in ("ga", "gb"):
        return "w_gates", [(k, (0 if kind == "ga" else 8) + c) for k, c in two]
    if kind in ("wa", "wb"):
        return {"wa": "w_a_out", "wb": "w_b_out"}[kind], two
    if kind in ("wo", "w2"):
        every = [(k, c) for k in range(4) for c in range(KT)]
        every += [(k, c) for q in range(4) for k in range(4, KT) for c in (2 * q, 2 * q + 1)]
        return {"wo": "w_o", "w2": "w_out_2"}[kind], every[16 * j:16 * j + 16]
    if kind == "u1":
        return "w_up", [(k, c) for k in range(KT) for c in (j, FF1 + j)]
    if kind == "d1":
        every = [(k, c) for g in (0, 8) for q in range(4) for k in range(g, g + 8) for c in (2 * q, 2 * q + 1)]
        every += [(k, c) for c in range(KT) for k in range(16, FF1)]
        return "w_down", every[16 * j:16 * j + 16]
    if kind in COL2:
        return "w_in_2", [(k, COL2[kind] + c) for k, c in two]
    if kind == "pa":
        return "w_proj_a_2", [(k, c) for c in range(4 * j, 4 * j + 4) for k in range(4)]
    if kind == "pb":
        return "w_proj_b_2", [(8 * (j % 2) + k, 2 * (j // 2) + c) for k in range(8) for c in range(2)]
    if kind == "u2":
        return "w_up_2", two
    return "w_down_2", [(8 * (j // 4) + k, 2 * (j % 4) + c) for k in range(8) for c in range(2)]


PAR = {}
_at = 0
for _name, _n in (("g_mix", 8), ("conv_a", 24), ("conv_g", 96), ("g_ffn", 8), ("conv_f", 132), ("g_fin", 8),
                  ("g_n1", 8), ("g_q", 12), ("g_k", 12), ("gn_g", 16), ("gn_b", 16), ("g_n2", 8),
                  ("g_o", 1), ("a_log", 1), ("dt_b", 1), ("eps", 1), ("one", 1), ("ln_scale", 1),
                  ("ident", 128), ("ones", 128)):
    PAR[_name] = _at
    _at += _n
NPAR = _at
CHUNK = 64

ACCUM = ("wo", "d1", "pa", "w2", "d2")
RING = [key for key in SEQ if key[0] not in ACCUM and not (key[0] == "pb" and key[1] % 2 == 0)]
GRP = {key: g for g, key in enumerate(RING)}
EARLY = {("wo", 2): 7, ("wo", 3): 7, ("d1", 10): 3, ("w2", 2): 7, ("w2", 3): 7}
HALF = {key: i + 1 for i, key in enumerate(EARLY)}
for _j in range(0, 8, 2):
    GRP[("pb", _j)] = GRP[("pb", _j + 1)]


def schedule():
    todo = {n: [] for n in range(-1, NB)}

    def put(n, step, *a):
        todo[n].append((step, a))

    put(-1, "x0")
    put(0, "norm", 0)
    for i, kind in enumerate("kqv"):
        for j in range(4):
            n = AT[(kind, j)]
            put(n, "tap4", kind, j)
            put(n + 1, "conv4", kind, j)
            put(n + 1, "silu", kind, j)
            if kind != "v":
                if j % 2:
                    put(n + 2, "l2n", kind, j - 1)
                    put(n + 2, "l2n", kind, j)
    put(3, "ab_mm")
    put(4, "ab_gates")
    put(5, "ab_decay")
    put(7, "ab_tok")
    put(8, "ab_cum")
    for h in range(0, H1, 2):
        n = 10 + h // 2
        for i in (h, h + 1):
            put(n, "rows", i)
        for i in (h, h + 1):
            put(n + 2, "kk", i)
    for b in range(4):
        put(15 + b, "tok", b)
    put(17, "lev0")
    put(18, "lev0t")
    for l in range(5):
        put(19 + l, "level", l)
    put(24, "uw")
    put(25, "state", 0)
    put(26, "wstate", 1)
    put(27, "state", 1)
    put(28, "wstate", 2)
    put(29, "state", 2)
    put(29, "o", 0)
    put(30, "wstate", 3)
    put(31, "o", 1)
    for q in range(4):
        put(31 + q // 2, "osq", q)
        put(33 + q // 2, "onorm", q)
    for j in range(4):
        n = AT[("x", j)]
        put(n, "gatec", j)
        put(n + 1, "mixc", j)
        put(AT[("ga", j)], "sig", "ga", j)
        n = AT[("gb", j)]
        put(n + 1, "sig", "gb", j)
    for j in range(4):
        n = AT[("z", j)]
        put(n, "zg", j)
        put(AT[("wb", j)], "mix", j)
        put(AT[("wo", 2 + j // 2)], "res1", j)
    put(AT[("wb", 0)], "xres")
    put(AT[("wo", 3)] + 1, "norm", 1)
    for j in range(FF1):
        n = AT[("u1", j)]
        put(n, "conv3", j)
        put(n + 1, "ffn1", j)
    for step, q, j in (("res2", 0, 8), ("sum2", 0, 8), ("res2", 1, 9), ("res2", 2, 10), ("sum2", 1, 10), ("res2", 3, 10),
                       ("sum2", 2, 10), ("sum2", 3, 10)):
        put(AT[("d1", j)], step, q)
    put(AT[("d1", 10)] + 1, "norm", 2)
    for kind in ("qa", "ka"):
        for j in range(6):
            n = AT[(kind, j)]
            put(n, "sqh", kind, j)
            put(n + 1, "rmsh", kind, j)
    put(AT[("ka", 0)], "x2")
    put(AT[("qa", 1)], "rtok")
    n = AT[("kr", 0)]
    for i in range(10):
        if i < 8:
            put(n + i, "att_s", i)
        if 1 <= i < 9:
            put(n + i, "att_t", i - 1)
        if i >= 2:
            put(n + i, "att_o", i - 2)
    n = AT[("vr", 2)]
    for h in range(RH):
        put(n + h, "ret_s", h)
    for i in range(8):
        put(AT[("gr", i)] + 1, "silur", i)
    n = AT[("gr", 3)]
    for i in range(10):
        if i < 8:
            put(n + i, "ret_o", i)
        if i >= 2:
            put(n + i, "ret_x", i - 2)
        if 1 <= i < 9:
            put(n + i, "ret_t", i - 1)
    for kind in ("ta", "tb"):
        for j in range(4):
            put(AT[(kind, j)], "sig", kind, j)
    put(AT[("pa", 1)], "ma")
    for j in range(4):
        put(AT[("pb", 2 * j + 1)], "mix2", j)
        put(AT[("w2", 2 + j // 2)], "res3", j)
    put(AT[("w2", 3)] + 1, "norm", 3)
    for j in range(16):
        put(AT[("u2", j)], "ffn2", j)
    for q in range(4):
        put(AT[("d2", 12 + q)], "res4", q)
    return todo


TODO = schedule()
URGENT = {n for n, (kind, j) in enumerate(SEQ) if kind in ("wb", "wo", "w2") or (kind == "d1" and j > 7)} | {
    0, AT[("wo", 3)] + 1, AT[("d1", 10)] + 1, AT[("w2", 3)] + 1}
POOL_LOW = {AT[("x", 0)], AT[("c", 1)], AT[("wo", 2)] + 3, AT[("w2", 2)] + 3}
ORDER = [item for n in range(-1, NB) for item in TODO[n]]
OWN = {"gatec": ("x",), "conv3": ("u1",)}
SIG = {a: i for i, a in enumerate([o[1] for o in ORDER if o[0] == "sig"])}
SILU = {a: i for i, a in enumerate([o[1] for o in ORDER if o[0] == "silu"])}
CONV, TAPS = {}, {}
_n = 0
for _step, _a in ORDER:
    if _step in ("tap4", "gatec", "conv3"):
        _a = OWN.get(_step, ()) + _a
        CONV[_a] = len(CONV)
        _n += 6 if _step == "tap4" else 4
        TAPS[_a] = _n
CONV_KEY = {i: a for a, i in CONV.items()}
HEADN = {a: i for i, (_, a) in enumerate([o for o in ORDER if o[0] in ("l2n", "onorm", "rmsh")])}


SEMS = """
ab abT aba abh abl abv abw am ao as at bag bs bst cum cv cx dec dr dt eg ev f1 f1h f2 f2h fp fq2 fs g2 g2z g3
gc gg gs gtok h h0 half hln hsum kb kk kn lt m2 m20 m2h ma mask mc md mm ms ms0 mx mx0 mxh nl nm nsum o oa oah oc
og ogh on onr or orh out pa_ par pb_ pc pe pn pt qd qk r1 r2 r3 raw0 raw1 rawh rb rd res4 rg ri rl ro row rr rs rsp rt rtT
rtk rtp ry s0 sc sel sg silu sp sq sq0 sqh sqp sqr sr ss ss0 ssa st t0 t0c tap tb tk tok tsa uw uwp vn wh wh0 wl wl0 ws x0 x0h
x1 x1h x2 x3 x3h xT xTb xb xbh xres ya yah zp zs
""".split()


def program(nc, wts, par_d, x_d, abw_d, sums_d, mask_d, sel_d, md_d, dr_d, out_d):
    with ExitStack() as ctx:
        def sb(name, shape, dt=F32, own=None):
            return (own or ctx).enter_context(nc.sbuf_tensor(name, shape, dt))

        sem = {name: ctx.enter_context(nc.semaphore("s_" + name)) for name in SEMS}
        raw = sb("raw", [P, 2, 16, P])
        wh = sb("wh", [P, 3, 16, P], F32R)
        wl = sb("wl", [P, 3, 16, P], F32R)
        Yh, Yl = sb("Yh", [P, KT, S], F32R), sb("Yl", [P, KT, S], F32R)
        xT = sb("xT", [P, KT, S])
        par = sb("par", [P, NPAR])
        rb, rfin, lnt = sb("rb", [P, S]), sb("rfin", [P, S]), sb("lnt", [P, S])
        y = [sb(f"y{i}", [P, 2, S]) for i in range(2)]
        acc = [sb(f"acc{i}", [P, 2, S]) for i in range(2)]
        e = [sb(f"e{i}", [P, 2, S]) for i in range(2)]
        t2 = [sb(f"t2{i}", [P, 2, S]) for i in range(2)]
        sq = [sb(f"sq{i}", [P, 2, S]) for i in range(2)]
        onesr = sb("onesr", [P, P], F32R)
        ss = [sb(f"ss{i}", [P, 2, S]) for i in range(2)]
        small = sb("small", [P, 64])
        rtok = sb("rtok", [P, 2])
        with ExitStack() as own:
            Xh, Xl = sb("Xh", [P, KT, S], F32R, own), sb("Xl", [P, KT, S], F32R, own)
        xf = sb("xf", [P, 4096])
        dr = xf[:, 2048:3072].rearrange("p (h i) -> p h i", h=4)
        md = xf[:, 3072:3840].rearrange("p (g i) -> p g i", g=3)
        ST = [xf[:, a:a + 384] for a in (0, 384, 1024, 1408)]
        with ExitStack() as own:
            ga_ = sb("gdn", [P, 8, KT, S], F32, own)
        with ExitStack() as own:
            sb("below", [P, 4, KT, S], F32, own)
            abh, abl = sb("abh", [P, KT, 64], F32R, own), sb("abl", [P, KT, 64], F32R, own)
        with ExitStack() as own:
            Zh, Zl = sb("Zh", [P, KT, S], F32R, own), sb("Zl", [P, KT, S], F32R, own)
        sc = sb("mix2", [P, 16384])
        with ExitStack() as own:
            cg, bg = sb("cg", [P, 2, S], F32, own), sb("bg", [P, 2, S], F32, own)
            G2, abt = sb("G2", [64, S], F32, own), sb("abt", [64, 3, S], F32, own)
        Oh, Ol = sb("Oh", [P, 4, S], F32R), sb("Ol", [P, 4, S], F32R)

        def full(i):
            return ga_[:, i]

        def tiles(i):
            return ga_[:, i].rearrange("p h (t m) -> p h t m", t=2)

        qn, kn, vv, kb, qd, DT, LT, AQ = (full(i) for i in range(8))
        SI, KD, VB, TI, KBE, U, WT, OT = (tiles(0), tiles(1), tiles(2), tiles(3), tiles(5), tiles(6), tiles(3), full(5))
        sgb, xres = full(0), full(3)
        hist = [ga_[:, 0, 0:4].rearrange("p a (b m) -> p (a b) m", b=2),
                ga_[:, 0, 4:8].rearrange("p a (b m) -> p (a b) m", b=2),
                ga_[:, 2, 0:4].rearrange("p a (b m) -> p (a b) m", b=2)]
        dec = ga_[:, 2, 4:8].rearrange("p a (b m) -> p (a b) m", b=2)
        m1 = xT
        sel = xT[:, 0:4].rearrange("p a (b m) -> p (a b) m", b=2)
        sums = xT[:, 5:8].rearrange("p a (b m) -> p (a b) m", b=2)[:, 0:5]
        negm, tri, blk, cm = sums[:, 0], sums[:, 1], sums[:, 2], (sums[:, 3], sums[:, 4])
        mask = xT[:, 0:3].rearrange("p a (b m) -> p (a b) m", b=2)
        abw = ga_[:, 5, 0:2].rearrange("p a (b m) -> p (a b) m", b=4)
        atn = sb("atn", [P, 2, 4])
        bst, bag, rsd = sb("bst", [P, 2, 6]), sb("bag", [P, 2, 2]), sb("rsd", [P, 2, 2])
        G3 = xT[0:8, 4]
        den = xT[0:64, 4]
        gtok = sb("gtok", [P, 2, 40])
        TS = sb("TS", [P, 5, H1, 2])
        egl = sb("egl", [P, 4, H1])
        Gs = sb("Gs", [P, 64])

        def part(kb_, n, **kw):
            return sc[:, 256 * kb_:256 * (kb_ + n)].rearrange("p (a i) -> p a i", **kw)

        att_s = [part(3 * i, 3, a=3) for i in range(2)]
        att_p = [part(6 + 3 * i, 3, a=6) for i in range(2)]
        qr, qa, ka, kr = part(12, 8, a=8), part(20, 12, a=12), part(32, 12, a=12), part(56, 8, a=8)
        va = part(44, 12, a=2)
        vr = part(20, 16, a=2)
        gr = part(36, 16, a=16)
        ta = part(52, 8, a=8)

        def tb(j):
            return part(60 + 2 * j, 2, a=2) if j < 2 else part(12 + 2 * j, 2, a=2)

        psS = [ctx.enter_context(nc.psum_tensor(f"psS{i}", [P, 2, S], F32)) for i in range(2)]
        psA = [ctx.enter_context(nc.psum_tensor(f"psA{i}", [P, 2, S], F32)) for i in range(6)]

        def flat(b):
            return psA[b][:].rearrange("p a b -> p (a b)")

        def quad(b):
            return psA[b][:].rearrange("p a (c m) -> p (a c) m", m=P)

        def pcol(name, i=0, lo=0, hi=P):
            return par[lo:hi, PAR[name] + i:PAR[name] + i + 1]

        ident = par[:, PAR["ident"]:PAR["ident"] + P]
        ones = par[:, PAR["ones"]:PAR["ones"] + P]
        gg = small[:, 0:8]

        def two(ap):
            return ap.unsqueeze(1).broadcast_to([P, 2, S])

        def f32(ap):
            return ap.bitcast(F32)

        def ring(key):
            return psS[GRP[key] % 2]

        def pair(t, j):
            return t[:, 2 * j:2 * j + 2]

        GDST = {"ta": lambda j: pair(ta, j), "tb": tb, "gb": lambda j: pair(sgb, j)}
        QK = {"qa": qa, "ka": ka}
        QKV = {"q": qn, "k": kn, "v": vv}
        YKINDS = ("k", "q", "v", "x", "ga", "gb", "z", "u1", "gr", "ta", "tb")

        def yk(key):
            return y[AT[key] % 2]

        def hbank(i):
            return psA[2 + i % 2] if i < 8 else psA[i % 2]

        block = ctx.enter_context(nc.Block())

        @block.sync
        def _(sp):
            sp.dma_start(par[:], par_d).then_inc(sem["par"], 16)
            sp.dma_start(xT[:, 0:4], x_d[:, 0:4]).then_inc(sem["xT"], 16)
            sp.dma_start(raw[:, 0, 0:8], wts[0][:, 0:8]).then_inc(sem["rawh"], 16)
            sp.dma_start(xT[:, 4:8], x_d[:, 4:8]).then_inc(sem["xTb"], 16)
            sp.dma_start(raw[:, 0, 8:16], wts[0][:, 8:16]).then_inc(sem["raw0"], 16)

            def load(n):
                if n >= 2:
                    sp.wait_ge(sem["wl"], n - 1)
                sp.dma_start(raw[:, n % 2], wts[n]).then_inc(sem[f"raw{n % 2}"], 16)

            load(1)
            sp.dma_start(abw, abw_d).then_inc(sem["abw"], 16)
            for n in range(2, NB):
                load(n)
                if n == 3:
                    sp.wait_ge(sem["ss"], 1)
                    sp.wait_ge(sem["x0"], KT)
                    sp.dma_start(sel, sel_d).then_inc(sem["sel"], 16)
                    sp.dma_start(sums, sums_d).then_inc(sem["gc"], 16)
                if n == AT[("x", 2)]:
                    sp.wait_ge(sem["row"], 8)
                    sp.dma_start(mask, mask_d).then_inc(sem["mask"], 16)
                if n == AT[("wb", 2)]:
                    sp.wait_ge(sem["vn"], 6)
                    sp.dma_start(xres, x_d).then_inc(sem["xres"], 16)
                if n == AT[("ka", 0)]:
                    sp.wait_ge(sem["mm"], AT[("d1", 10)] + 1)
                    sp.dma_start(xf[:, 2048:3072], dr_d).then_inc(sem["dr"], 16)
                    sp.dma_start(xf[:, 3072:3840], md_d).then_inc(sem["md"], 16)
            for q in range(4):
                sp.wait_ge(sem["res4"], q + 1)
                sp.dma_start(pair(out_d, q), pair(xT, q)).then_inc(sem["out"], 16)
            sp.wait_ge(sem["out"], 64)

        @block.tensor
        def _(pe):
            OPER = {}
            for kind in COL1:
                OPER[kind] = (Xh, Xl, "x0", lambda k: k + 1)
            OPER["ga"] = OPER["gb"] = OPER["x"]
            OPER["wa"] = (Yh, Yl, "ya", lambda k: k // 2 + 1)
            OPER["wb"] = (Yh, Yl, "og", lambda k: k // 2 + 1)
            OPER["wo"] = (Xh, Xl, "mx", lambda k: k // 2 + 1)
            OPER["u1"] = (Yh, Yl, "x1", lambda k: k + 1)
            for kind in COL2:
                OPER[kind] = (Yh, Yl, "xb", lambda k: k + 1)
            OPER["w2"] = (Yh, Yl, "m2", lambda k: k // 2 + 1)
            OPER["u2"] = (Xh, Xl, "x3", lambda k: k + 1)

            def operand(kind, k):
                if kind == "d1":
                    h, l = ((Xh, Xl), (Zh, Zl), (Xh, Xl))[k // 8]
                    return h, l, k % 8, "f1", k + 1
                if kind == "d2":
                    h, l = ((Yh, Yl), (Zh, Zl))[k // 8 % 2]
                    return h, l, k % 8, "f2", k // 2 + 1
                if kind == "pa":
                    return Oh, Ol, k, "oa", 8
                if kind == "pb":
                    h, l = ((Zh, Zl), (Xh, Xl))[k // 8]
                    return h, l, k % 8, "or", 2 * (k // 4) + 2
                h, l, s, v = OPER[kind]
                return h, l, k, s, v(k)

            def stream(n):
                kind, j = SEQ[n]
                beside = [(step, a + part) for step, a in TODO[n - 1] if step in steps
                          for part in (((b,) for b in range(8)) if step == "level" else ((),))]
                at = [16 * (i + 1) // (len(beside) + 1) for i in range(len(beside))]
                if beside and beside[0][0] == "norm":
                    at[0] = 7
                if n:
                    pe.wait_ge(sem["wl"], n + 1)
                else:
                    pe.wait_ge(sem["wl0"], 1)
                key = (kind, j)
                fresh = True
                if key in RING or kind == "pb":
                    fresh = not (kind == "pb" and j % 2)
                    if fresh and GRP[key] >= 2:
                        pe.wait_ge(sem["ev"], GRP[key] - 1)
                if kind == "pa":
                    pe.wait_ge(sem["rt"], 8)
                if j == 0 and kind in ("wo", "d1", "w2", "d2"):
                    pe.wait_ge(*{"wo": (sem["og"], 4), "d1": (sem["r1"], 4), "w2": (sem["ma"], 4),
                                 "d2": (sem["r3"], 4)}[kind])
                _, prs = pairs(kind, j)
                seen = set()
                begun = set()
                for p, (k, c) in enumerate(prs):
                    for (step, a), place in zip(beside, at):
                        if place == p:
                            steps[step](*a)
                    if n == 0 and p == 8:
                        pe.wait_ge(sem["wl"], 1)
                    h, l, kk_, s, v = operand(kind, k)
                    if k not in seen:
                        pe.wait_ge(sem[s], v)
                        seen.add(k)
                    if kind in ("va", "vr"):
                        if p % 2:
                            continue
                        w = [t[:, n % 3].rearrange("p a b -> p (a b)")[:, p * P:(p + 2) * P] for t in (wh, wl)]
                        for t in range(2):
                            o = ring(key)[:, t]
                            for i, (a, b) in enumerate(((h, w[0]), (l, w[0]), (h, w[1]))):
                                mm = pe.matmul(o, a[:, kk_, t * P:(t + 1) * P], b,
                                               start=(p == 0 and t == 0 and i == 0), stop=(p == 14 and i == 2),
                                               skip_group_check=True)
                        continue
                    if kind in ACCUM:
                        bank, half = psA[c // 2], c % 2
                    else:
                        bank, half = ring(key), p % 2
                    first = k == 0 and c % 2 == 0 if kind in ACCUM else fresh and p == 0
                    last = {"wo": k == KT - 1, "d1": k == FF1 - 1, "w2": k == KT - 1, "d2": k == 31, "pa": k == 3,
                            "pb": j % 2 == 1 and p >= 14}.get(kind, p >= 14)
                    for i, (a, b) in enumerate(((wh, h), (wh, l), (wl, h))):
                        mm = pe.matmul(bank[:, half], a[:, n % 3, p, :], b[:, kk_, :], start=(first and i == 0),
                                       stop=(last and i == 2), skip_group_check=True)
                    if EARLY.get((kind, j)) == p:
                        mm.then_inc(sem["half"], 1)
                mm.then_inc(sem["mm"], 1)

            def norm(i):
                pe.wait_ge(sem["ss"], i + 1)
                if i:
                    pe.wait_ge(sem["rb"], i)
                for g in range(2 if i == 2 else 1):
                    for half in range(2):
                        mm = pe.matmul(psA[5][:, g], ones, ss[g][:, half], start=(half == 0), stop=(half == 1),
                                       skip_group_check=True)
                mm.then_inc(sem["nsum"], 1)

            def ab_mm():
                pe.wait_ge(sem["abl"], 1)
                for k in range(KT):
                    for i, (a, b) in enumerate(((abh, Xh), (abh, Xl), (abl, Xh))):
                        mm = pe.matmul(psA[4][0:64, 0], a[:, k], b[:, k], start=(k == 0 and i == 0),
                                       stop=(k == KT - 1 and i == 2))
                mm.then_inc(sem["ab"], 1)

            def ab_tok():
                pe.wait_ge(sem["g2"], 2)
                for t in range(2):
                    mm = pe.transpose(psA[4][:, 0, 40 * t:40 * t + 40], G2[0:40, t * P:(t + 1) * P],
                                      ident[0:40, 0:40])
                mm.then_inc(sem["abT"], 1)

            def ab_cum():
                pe.wait_ge(sem["gtok"], 1)
                pe.wait_ge(sem["gc"], 16)
                q = flat(4)
                for t in range(2):
                    g = gtok[:, t, 0:8]
                    outs = ((tri, 8 * t), (blk, 16 + 8 * t), (cm[0], 32 + 16 * t), (cm[1], 40 + 16 * t))
                    for a, o in outs:
                        pe.matmul(q[:, o:o + 8], a, g, start=True, stop=True)
                for t in range(2):
                    mm = pe.matmul(psA[4][0:8, 1, t * P:(t + 1) * P], gtok[:, t, 0:8], tri, start=True, stop=True)
                mm.then_inc(sem["cum"], 1)

            def colsum(i, bank, src, count):
                pe.wait_ge(sem["sq"], count)
                pe.matmul(psA[bank][:], ones, src, start=True, stop=True).then_inc(sem["hsum"], 1)

            def l2n(kind, j):
                i = HEADN[(kind, j)]
                if i >= 2:
                    pe.wait_ge(sem["hln"], i - 1)
                colsum(i, 2 + i % 2, sq[i % 2][:], i + 1)

            def colsum2(i):
                pe.wait_ge(sem["sq"], i + 1)
                pe.wait_ge(sem["onr"], 1)
                pe.matmul(psA[i % 2][:], onesr[:], pair(Zh, i % 2), start=True, stop=False)
                pe.matmul(psA[i % 2][:], onesr[:], pair(Zl, i % 2), start=False, stop=True).then_inc(sem["hsum"], 1)

            def onorm(q):
                i = HEADN[(q,)]
                if q < 2:
                    pe.wait_ge(sem["vn"], 6)
                pe.wait_ge(sem["hln"], i - 1)
                colsum(i, q % 2, sq[i % 2][:], i + 1)

            def rmsh(kind, j):
                i = HEADN[(kind, j)]
                pe.wait_ge(sem["hln"], i - 1)
                if i == 12:
                    pe.wait_ge(sem["xb"], 8)
                colsum2(i)

            def rows(h):
                if h == 0:
                    pe.wait_ge(sem["sel"], 16)
                    pe.wait_ge(sem["g3"], 1)
                if h >= 2:
                    pe.wait_ge(sem["eg"], h - 1)
                pe.matmul(psA[4 * (h % 2)][:, 0], sel[32:40, h], G2[32:40, :], start=True, stop=True)
                pe.matmul(psA[4 * (h % 2) + 1][:, 1], sel[0:8, h], G3, start=True, stop=True).then_inc(sem["row"], 1)

            def kk(h):
                if h == 0:
                    pe.wait_ge(sem["kn"], 8)
                    pe.wait_ge(sem["hln"], 8)
                pe.wait_ge(sem["kb"], 2 * h + 1)
                if h >= 2:
                    pe.wait_ge(sem["lt"], 2 * h - 2)
                for t in range(2):
                    s = slice(t * P, (t + 1) * P)
                    pe.matmul(quad(2 + h % 2)[:, 2 * t], kn[:, h, s], kb[:, h, s], start=True, stop=True)
                    mm = pe.matmul(quad(2 + h % 2)[:, 2 * t + 1], kn[:, h, s], qn[:, h, s], start=True, stop=True)
                mm.then_inc(sem["kk"], 1)

            def tok(b):
                if b == 0:
                    pe.wait_ge(sem["silu"], 12)
                    pe.wait_ge(sem["eg"], 8)
                if b:
                    pe.wait_ge(sem["tok"], 3 * b)
                for src, bank in ((kn, 4), (vv, 5)):
                    for i in range(4):
                        mm = pe.transpose(quad(bank)[:, i], src[:, 2 * b + i // 2, i % 2 * P:(i % 2 + 1) * P], ident)
                    mm.then_inc(sem["tk"], 1)

            def lev0t():
                pe.wait_ge(sem["eg"], 8)
                pe.wait_ge(sem["lt"], 16)
                for b in range(4):
                    pe.wait_ge(sem["s0"], 2 * b + 2)
                    for i in range(4):
                        mm = pe.transpose(quad(b)[:, i], SI[:, 2 * b + i // 2, i % 2], ident)
                    mm.then_inc(sem["t0"], 1)

            def level(l, part):
                def left(b):
                    i = 4 * l + b
                    pe.wait_ge(sem["bs"], i + 1)
                    if l == 0:
                        pe.wait_ge(sem["t0c"], b + 1)
                        if b < 2:
                            pe.wait_ge(sem["tok"], 12)
                    else:
                        pe.wait_ge(sem["st"], 2 * (i - 4) + 2)
                    if i >= 2:
                        pe.wait_ge(sem["pc"], i - 1)
                    for q in range(4):
                        mm = pe.matmul(quad(4 + b % 2)[:, q], sq[b % 2][:].rearrange("p a (c m) -> p (a c) m", m=P)[:, q],
                                       TI[:, 2 * b + q // 2, q % 2], start=True, stop=True)
                    mm.then_inc(sem["pa_"], 1)

                def right(b):
                    i = 4 * l + b
                    pe.wait_ge(sem["pc"], i + 1)
                    if l == 0:
                        pe.wait_ge(sem["t0c"], 4)
                    if i >= 2:
                        pe.wait_ge(sem["st"], 2 * (i - 2) + 2 if i - 2 < 16 else 32 + i - 17)
                    pb = ss[b % 2][:].rearrange("p a (c m) -> p (a c) m", m=P)
                    for q in range(4):
                        s = SI[:, 2 * b + q // 2, q % 2]
                        mm = pe.matmul(quad(2 * (b % 2))[:, q], pb[:, q], s, start=True, stop=True)
                    if l < 4:
                        for q in range(4):
                            s = SI[:, 2 * b + q // 2, q % 2]
                            mm = pe.matmul(quad(2 * (b % 2) + 1)[:, q], s, pb[:, q], start=True, stop=True)
                    mm.then_inc(sem["pb_"], 1)

                side, b = ((left, 0), (left, 1), (right, 0), (left, 2), (right, 1), (left, 3), (right, 2), (right, 3))[part]
                side(b)

            def uw():
                for b in range(4):
                    pe.wait_ge(sem["st"], 32 + (4 if b < 2 else b + 1))
                    if b >= 2:
                        pe.wait_ge(sem["uw"], 2 * (b - 2) + 2)
                    for q in range(4):
                        mm = pe.matmul(quad(2 * (b % 2))[:, q], SI[:, 2 * b + q // 2, q % 2],
                                       VB[:, 2 * b + q // 2, q % 2], start=True, stop=True)
                    for q in range(4):
                        mm = pe.matmul(quad(2 * (b % 2) + 1)[:, q], KBE[:, 2 * b + q // 2, q % 2],
                                       SI[:, 2 * b + q // 2, q % 2], start=True, stop=True)
                    mm.then_inc(sem["uwp"], 1)

            def state(c):
                t, r = c // 2, slice(CHUNK * (c % 2), CHUNK * (c % 2) + CHUNK)
                if c == 0:
                    pe.wait_ge(sem["uw"], 8)
                    pe.wait_ge(sem["pc"], 20)
                else:
                    pe.wait_ge(sem["vn"], 2 * c)
                    pe.wait_ge(sem["h0"], 2) if c == 1 else pe.wait_ge(sem["h"], 2 * c - 2)
                for h in range(H1):
                    mm = pe.matmul(quad(4 + h // 4)[:, h % 4], KD[r, h, t], U[r, h, t], start=True, stop=True)
                mm.then_inc(sem["sp"], 1)

            def wstate(c):
                t = c // 2
                pe.wait_ge(sem["h0"], 2) if c == 1 else pe.wait_ge(sem["h"], 2 * c - 2)
                if c > 1:
                    pe.wait_ge(sem["vn"], 2 * c - 2)
                for h in range(H1):
                    mm = pe.matmul(quad(h // 4)[:, h % 4], WT[:, h, t], hist[c - 1][:, h], start=True, stop=True)
                mm.then_inc(sem["ws"], 1)

            def o(t):
                pe.wait_ge(sem["vn"], 4 * t + 2)
                pe.wait_ge(sem["h"], 4 * t) if t else pe.wait_ge(sem["h0"], 2)
                if t:
                    pe.wait_ge(sem["oc"], 2)
                for h in range(H1):
                    dst = quad(2 + h // 4)[:, h % 4]
                    mm = pe.matmul(dst, U[:, h, t], AQ[:, h, t * P:(t + 1) * P], start=True, stop=False,
                                   skip_group_check=True)
                    for c in (2 * t, 2 * t + 1):
                        if c:
                            lo = CHUNK * (c % 2)
                            mm = pe.matmul(dst[:, lo:lo + CHUNK], hist[c - 1][:, h],
                                           qd[:, h, c * CHUNK:(c + 1) * CHUNK], start=False,
                                           stop=(c % 2 == 1), skip_group_check=True)
                    if h % 4 == 3:
                        mm.then_inc(sem["o"], 1)

            def rtok_():
                pe.wait_ge(sem["rb"], 3)
                for t in range(2):
                    mm = pe.matmul(flat(4)[:, t:t + 1], rb[0:1, t * P:(t + 1) * P], ones[0:1, 0:1],
                                   start=True, stop=True)
                mm.then_inc(sem["rtp"], 1)

            def att_s_(i):
                hp, t = i // 2, i % 2
                n = P * (t + 1)
                if i == 0:
                    pe.wait_ge(sem["qk"], 24)
                if i >= 2:
                    pe.wait_ge(sem["sc"], 3 * (i - 1))
                for g in range(3):
                    h = 4 * g + hp
                    dst = flat(0)[:, g * P:(g + 1) * P] if t == 0 else psA[2 + g // 2][:, g % 2]
                    mm = pe.matmul(dst, qa[:, h, t * P:(t + 1) * P], ka[:, h, 0:n], start=True, stop=True)
                mm.then_inc(sem["as"], 1)

            def att_t(i):
                t = i % 2
                pe.wait_ge(sem["pn"], i + 1)
                if i:
                    pe.wait_ge(sem["pt"], i)
                for g in range(3):
                    for jt in range(t + 1):
                        q = g * (t + 1) + jt
                        mm = pe.transpose(quad(4 + q // 4)[:, q % 4], att_s[i % 2].rearrange("p a (c m) -> p (a c) m", m=P)[:, q], ident)
                mm.then_inc(sem["at"], 1)

            def att_o(i):
                hp, t = i // 2, i % 2
                pe.wait_ge(sem["pt"], i + 1)
                if i:
                    pe.wait_ge(sem["oa"], i)
                n = 3 * (t + 1)
                for q in range(n):
                    g, jt = q // (t + 1), q % (t + 1)
                    h = 4 * g + hp
                    mm = pe.matmul(quad(1)[:, 0], va[:, jt, h * P:(h + 1) * P], att_p[i % 2][:, q],
                                   start=(q == 0), stop=(q == n - 1))
                mm.then_inc(sem["ao"], 1)

            def ret_s(h):
                if h == 0:
                    pe.wait_ge(sem["sc"], 24)
                if h >= 2:
                    pe.wait_ge(sem["rs"], 2 * h - 2)
                b = 2 * (h % 2)
                for a in range(2):
                    pe.matmul(psA[b][:, 0], kr[:, 2 * h + a, 0:P], qr[:, 2 * h + a, :], start=(a == 0), stop=(a == 1))
                for a in range(2):
                    mm = pe.matmul(psA[b][:, 1, 0:P], kr[:, 2 * h + a, P:S], qr[:, 2 * h + a, P:S],
                                   start=(a == 0), stop=(a == 1))
                mm.then_inc(sem["rsp"], 1)

            def ret_o(i):
                h, t = i // 2, i % 2
                if i == 0:
                    pe.wait_ge(sem["rs"], 8)
                    pe.wait_ge(sem["pt"], 8)
                if i >= 2:
                    pe.wait_ge(sem["ry"], i - 1)
                for a in range(t + 1):
                    lhs = ST[h][:, t * P:(t + 1) * P] if a == 0 else ST[h][:, 2 * P:3 * P]
                    mm = pe.matmul(psA[4 + i % 2][:], lhs, vr[:, a, h * 512:(h + 1) * 512], start=(a == 0), stop=(a == t))
                mm.then_inc(sem["ro"], 1)

            def ret_t(i):
                pe.wait_ge(sem["ry"], i + 1)
                if i >= 2:
                    pe.wait_ge(sem["rt"], i - 1)
                if i < 2:
                    pe.wait_ge(sem["oa"], 8)
                for f in range(4):
                    mm = pe.transpose(quad(i % 2)[:, f], acc[i % 2][:].rearrange("p a (c m) -> p (a c) m", m=P)[:, f],
                                      ident)
                mm.then_inc(sem["rtT"], 1)

            steps = {"norm": norm, "ab_mm": ab_mm, "ab_tok": ab_tok, "ab_cum": ab_cum, "l2n": l2n, "onorm": onorm,
                     "rmsh": rmsh, "rows": rows, "kk": kk, "tok": tok, "lev0t": lev0t, "level": level, "uw": uw,
                     "state": state, "wstate": wstate, "o": o, "rtok": rtok_, "att_s": att_s_, "att_t": att_t,
                     "att_o": att_o, "ret_s": ret_s, "ret_o": ret_o, "ret_t": ret_t}
            pe.wait_ge(sem["par"], 16)
            for n in range(NB):
                stream(n)

        @block.scalar
        def _(act):
            loaded = [None]

            def exp_ln():
                if loaded[0] != "exp_ln":
                    act.preload_act_table_set("natural_log_exp_and_others")
                loaded[0] = "exp_ln"

            def silu_():
                loaded[0] = "silu"
                return ACT.Silu

            def sigmoid_():
                loaded[0] = "sigmoid"
                return ACT.Sigmoid

            def split(n):
                act.wait_ge(sem[f"raw{n % 2}"], 16 * (n // 2 + 1))
                if n >= 3:
                    act.wait_ge(sem["mm"], n - 2)
                act.activation(wh[:, n % 3], raw[:, n % 2], ACT.Copy).then_inc(sem["wh"], 1)

            def high(dst, src, scale, name):
                act.activation(dst, src, ACT.Copy, scale=scale).then_inc(sem[name], 1)

            def x0():
                exp_ln()
                act.wait_ge(sem["par"], 16)
                for half, (x_there, w_there, done) in enumerate((("xT", "rawh", "wh0"), ("xTb", "raw0", "wh"))):
                    act.wait_ge(sem[x_there], 16)
                    for k in range(4 * half, 4 * half + 4):
                        high(Xh[:, k], xT[:, k], pcol("g_mix", k), "x0h")
                    act.wait_ge(sem[w_there], 16)
                    pairs_ = slice(8 * half, 8 * half + 8)
                    high(wh[:, 0, pairs_], raw[:, 0, pairs_], 1.0, done)

            def norm(i):
                exp_ln()
                act.wait_ge(sem["nsum"], i + 1)
                if i:
                    act.wait_ge(sem["rb"], i)
                act.activation(lnt[:], psA[5][:, 0], ACT.Ln, bias=pcol("eps"), scale=1.0 / D).then_inc(sem["nl"], 1)
                n = {0: 1, 1: 2, 2: 3, 3: 7}[i]
                act.wait_ge(sem["nl"], n)
                if i != 2:
                    if i:
                        act.wait_ge(sem[{1: "r1", 3: "r3"}[i]], 4)
                    act.activation(rb[:], lnt[:], ACT.Exp, scale=-0.5).then_inc(sem["rb"], 1)
                    return
                act.activation(rfin[:], lnt[:], ACT.Exp, scale=-0.5).then_inc(sem["nl"], 1)
                act.wait_ge(sem["ms"], 1)
                act.activation(lnt[:], lnt[:], ACT.Ln, bias=pcol("eps"), scale=1.0 / D).then_inc(sem["nl"], 1)
                act.wait_ge(sem["nl"], 5)
                act.activation(lnt[:], lnt[:], ACT.Exp, scale=-0.5).then_inc(sem["nl"], 1)

            def taps(a, w):
                i = CONV[a]
                if i >= 2:
                    b = CONV_KEY[i - 2]
                    if b[0] in QKV:
                        act.wait_ge(sem["silu"], SILU[b] + 1)
                    else:
                        act.wait_ge(sem["mc" if b[0] == "x" else "fp"], b[1] + 1)
                for f in range(2):
                    t = act.activation(acc[i % 2][:, f], yk(a)[:, f], ACT.Copy, scale=w[f])
                t.then_inc(sem["tap"], 1)

            def tap4(kind, j):
                act.wait_ge(sem["ev"], GRP[(kind, j)] + 1)
                c = {"q": 0, "k": 8, "v": 16}[kind] + 2 * j
                taps((kind, j), [pcol("conv_g", 72 + c + f) for f in range(2)])

            def gatec(j):
                act.wait_ge(sem["cx"], j + 1)
                taps(("x", j), [pcol("conv_a", 16 + 2 * j + f) for f in range(2)])

            def conv3(j):
                act.wait_ge(sem["ev"], GRP[("u1", j)] + 1)
                taps(("u1", j), [pcol("conv_f", 2 * 2 * FF1 + j + f * FF1) for f in range(2)])

            def silu(kind, j):
                act.wait_ge(sem["cv"], TAPS[(kind, j)])
                act.activation(pair(QKV[kind], j), acc[CONV[(kind, j)] % 2][:], silu_()).then_inc(sem["silu"], 1)

            def sig(kind, j):
                act.wait_ge(sem["ev"], GRP[(kind, j)] + 1)
                if kind == "ga":
                    if j >= 2:
                        act.wait_ge(sem["ev"], GRP[("wa", j - 2)] + 1)
                    dst = e[j % 2][:]
                else:
                    dst = GDST[kind](j)
                act.activation(dst, yk((kind, j))[:], sigmoid_()).then_inc(sem["sg"], 1)

            def zg(j):
                act.wait_ge(sem["ev"], GRP[("z", j)] + 1)
                if j >= 2:
                    act.wait_ge(sem["zp"], j - 1)
                act.activation(e[j % 2][:], yk(("z", j))[:], silu_()).then_inc(sem["zs"], 1)
                act.wait_ge(sem["zp"], j + 1)
                high(pair(Yh, j), t2[j % 2][:], 1.0, "ogh")

            def silur(j):
                act.wait_ge(sem["ev"], GRP[("gr", j)] + 1)
                act.activation(pair(gr, j), yk(("gr", j))[:], silu_()).then_inc(sem["sr"], 1)

            def ffn1(j):
                act.wait_ge(sem["cv"], TAPS[("u1", j)])
                if j >= 2:
                    act.wait_ge(sem["fp"], j - 1)
                act.activation(e[j % 2][:, 0], acc[CONV[("u1", j)] % 2][:, 0], silu_()).then_inc(sem["fs"], 1)
                act.wait_ge(sem["fp"], j + 1)
                high(((Xh, Zh, Xh)[j // 8])[:, j % 8], t2[j % 2][:, 1], 1.0, "f1h")

            def headnorm(i, scale, bias):
                exp_ln()
                act.wait_ge(sem["hsum"], i + 1)
                act.activation(t2[i % 2][:], hbank(i)[:], ACT.Ln, bias=pcol("eps"), scale=scale).then_inc(sem["hln"], 1)
                act.wait_ge(sem["hln"], i + 1)
                act.activation(t2[i % 2][:], t2[i % 2][:], ACT.Exp, scale=-0.5, bias=bias).then_inc(sem["ri"], 1)

            def l2n(kind, j):
                i = HEADN[(kind, j)]
                if i >= 2:
                    act.wait_ge(sem["kn"], i - 1)
                headnorm(i, 1.0, pcol("ln_scale") if kind == "q" else 0.0)

            def ab_mm():
                exp_ln()
                act.wait_ge(sem["abv"], 3)
                act.activation(abt[0:8, 0], abt[0:8, 2], ACT.Exp, scale=-1.0).then_inc(sem["aba"], 1)
                act.activation(abt[32:40, 0], abt[32:40, 0], ACT.Exp, scale=-1.0).then_inc(sem["aba"], 1)
                act.activation(small[0:8, 8:9], pcol("a_log", hi=8), ACT.Exp).then_inc(sem["aba"], 1)

            def ab_gates():
                exp_ln()
                act.wait_ge(sem["abv"], 4)
                act.activation(abt[0:8, 2], den[0:8], ACT.Ln).then_inc(sem["aba"], 1)

            def ab_cum():
                exp_ln()
                act.wait_ge(sem["gs"], 3)
                act.activation(TS[:, 4].rearrange("p h t -> p t h"), Gs[:, 0:16].rearrange("p (t h) -> p t h", t=2),
                               ACT.Exp).then_inc(sem["tsa"], 1)
                act.activation(TS[:, 3], TS[:, 3], ACT.Exp).then_inc(sem["tsa"], 1)
                act.activation(egl[:], Gs[:, 32:64].rearrange("p (c h) -> p c h", c=4), ACT.Exp).then_inc(sem["tsa"], 1)

            def rows(h):
                exp_ln()
                act.wait_ge(sem["kb"], 2 * h + 2)
                act.wait_ge(sem["kn"], 8) if h < 2 else act.wait_ge(sem["qd"], h - 1)
                act.activation(t2[h % 2][:, 0], psA[4 * (h % 2) + 1][:, 1], ACT.Exp).then_inc(sem["eg"], 1)
                if h == 0:
                    act.wait_ge(sem["gs"], 3)
                for t in range(2):
                    s = slice(t * P, (t + 1) * P)
                    a = act.activation(DT[:, h, s], DT[:, h, s], ACT.Exp, bias=TS[:, 0, h, t:t + 1])
                a.then_inc(sem["dt"], 1)

            def mixc(j):
                act.wait_ge(sem["mc"], j + 1)
                high(pair(Yh, j), t2[j % 2][:], 1.0, "yah")

            def lev0t():
                for b in range(4):
                    act.wait_ge(sem["t0"], b + 1)
                    act.activation(TI[:, 2 * b:2 * b + 2], psA[b][:].rearrange("p a (c m) -> p a c m", m=P),
                                   ACT.Copy).then_inc(sem["t0c"], 1)

            def level(l):
                for b in range(4):
                    i = 4 * l + b
                    act.wait_ge(sem["pa_"], i + 1)
                    if i >= 2:
                        act.wait_ge(sem["pb_"], i - 1)
                    act.activation(ss[b % 2][:], psA[4 + b % 2][:], ACT.Copy).then_inc(sem["pc"], 1)

            def uw():
                for b in range(4):
                    act.wait_ge(sem["uwp"], b + 1)
                    for i, dst in enumerate((U, WT)):
                        act.activation(dst[:, 2 * b:2 * b + 2],
                                       psA[2 * (b % 2) + i][:].rearrange("p a (c m) -> p a c m", m=P),
                                       ACT.Copy).then_inc(sem["uw"], 1)

            def state(c):
                if c == 0:
                    act.wait_ge(sem["sp"], 1)
                    for q in range(2):
                        act.activation(hist[0][:, 4 * q:4 * q + 4], quad(4 + q), ACT.Copy).then_inc(sem["h0"], 1)

            def o(t):
                for q in range(2):
                    act.wait_ge(sem["o"], 2 * t + q + 1)
                    act.activation(OT[:, 4 * q:4 * q + 4, t * P:(t + 1) * P], quad(2 + q), ACT.Copy).then_inc(sem["oc"], 1)

            def onorm(q):
                act.wait_ge(sem["on"], q - 1) if q >= 2 else act.wait_ge(sem["ya"], 4)
                headnorm(HEADN[(q,)], 1.0 / P, 0.0)

            def mix(j):
                act.wait_ge(sem["mx0"], j + 1)
                high(pair(Xh, j), t2[j % 2][:], 1.0, "mxh")

            def squares(i, j, gain):
                base = {1: 0, 2: 2, 3: 7}[i]
                per = 2 if i == 2 else 1
                if j == 3:
                    act.wait_ge(sem["ssa"], base + per)
                if j == 0:
                    act.wait_ge(sem["nsum"], i)
                dst, dstg = (sq[j % 2], t2[j % 2]) if j else ss
                act.activation(dst[:], pair(xT, j), ACT.Square).then_inc(sem["sqr"], 1)
                if i == 2:
                    for f in range(2):
                        a = act.activation(dstg[:, f], xT[:, 2 * j + f], ACT.Square, scale=pcol("g_fin", 2 * j + f))
                    a.then_inc(sem["sqr"], 1)

            def res1(j):
                act.wait_ge(sem["r1"], j + 1)
                for k in (2 * j, 2 * j + 1):
                    high(Yh[:, k], xT[:, k], pcol("g_ffn", k), "x1h")
                squares(1, j, None)

            def res2(j):
                act.wait_ge(sem["r2"], j + 1)
                for k in (2 * j, 2 * j + 1):
                    high(Yh[:, k], xT[:, k], gg[:, k:k + 1], "xbh")

            def sum2(j):
                squares(2, j, None)

            def res3(j):
                act.wait_ge(sem["r3"], j + 1)
                for k in (2 * j, 2 * j + 1):
                    high(Xh[:, k], xT[:, k], pcol("g_n2", k), "x3h")
                squares(3, j, None)

            def sqh(kind, j):
                act.wait_ge(sem["ev"], GRP[(kind, j)] + 1)
                i = HEADN[(kind, j)]
                act.wait_ge(sem["hsum"], i - 1)
                if i == 12:
                    act.wait_ge(sem["ss"], 3)
                act.activation(pair(Zh, i % 2), pair(QK[kind], j), ACT.Square).then_inc(sem["sqh"], 1)

            def rmsh(kind, j):
                i = HEADN[(kind, j)]
                if i == 12:
                    act.wait_ge(sem["ss"], 3)
                act.wait_ge(sem["qk"], 2 * (i - 12) - 2) if i >= 14 else None
                headnorm(i, 1.0 / P, 0.0)

            def att_s_(i):
                exp_ln()
                act.wait_ge(sem["nm"], i + 1)
                n = 3 * P * (i % 2 + 1)
                v = att_s[i % 2].rearrange("p a b -> p (a b)")[:, 0:n]
                act.activation(v, v, ACT.Exp, scale=SCALE, bias=atn[:, i % 2, 1:2],
                               accum_out=atn[:, i % 2, 2:3]).then_inc(sem["pe"], 1)

            def att_t(i):
                act.wait_ge(sem["at"], i + 1)
                if i >= 2:
                    act.wait_ge(sem["ao"], i - 1)
                if i % 2 == 0:
                    act.activation(att_p[0][:, 0:3], quad(4)[:, 0:3], ACT.Copy).then_inc(sem["pt"], 1)
                else:
                    act.activation(att_p[1][:, 0:4], quad(4), ACT.Copy)
                    act.activation(att_p[1][:, 4:6], quad(5)[:, 0:2], ACT.Copy).then_inc(sem["pt"], 1)

            def att_o(i):
                act.wait_ge(sem["ao"], i + 1)
                high(Oh[:, i // 2, i % 2 * P:(i % 2 + 1) * P], quad(1)[:, 0], 1.0, "oah")

            def ret_o(i):
                exp_ln()
                act.wait_ge(sem["bag"], i + 1)
                act.activation(rsd[:, i % 2, 0:1], bag[:, i % 2, 1:2], ACT.Ln, bias=pcol("eps")).then_inc(sem["rl"], 1)
                act.wait_ge(sem["rl"], i + 1)
                act.activation(rsd[:, i % 2, 1:2], rsd[:, i % 2, 0:1], ACT.Exp, scale=-0.5).then_inc(sem["rr"], 1)

            def ret_t(i):
                h, t = i // 2, i % 2
                act.wait_ge(sem["rtT"], i + 1)
                act.wait_ge(sem["or"], i - 1) if i >= 2 else act.wait_ge(sem["qk"], 24)
                y_ = t2[i % 2][:].rearrange("p a (c m) -> p (a c) m", m=P)
                for f in range(4):
                    a = act.activation(y_[:, f], quad(i % 2)[:, f], ACT.Identity, scale=pcol("gn_g", 4 * h + f),
                                       bias=pcol("gn_b", 4 * h + f))
                a.then_inc(sem["rt"], 1)

            def ret_x(i):
                h, t = i // 2, i % 2
                act.wait_ge(sem["rg"], i + 1)
                dst = (Zh, Xh)[h // 2][:, 4 * (h % 2):4 * (h % 2) + 4, t * P:(t + 1) * P]
                high(dst, t2[i % 2][:].rearrange("p a (c m) -> p (a c) m", m=P), 1.0, "orh")

            def mix2(j):
                act.wait_ge(sem["m20"], j + 1)
                high(pair(Yh, j), t2[j % 2][:], 1.0, "m2h")

            def ffn2(j):
                act.wait_ge(sem["ev"], GRP[("u2", j)] + 1)
                act.activation(pair((Yh, Zh)[j // 4 % 2], j % 4), y[j % 2][:], ACT.Square).then_inc(sem["f2h"], 1)

            steps = {"x0": x0, "norm": norm, "tap4": tap4, "gatec": gatec, "conv3": conv3, "silu": silu, "sig": sig,
                     "zg": zg, "silur": silur, "ffn1": ffn1, "l2n": l2n, "ab_mm": ab_mm, "ab_gates": ab_gates, "ab_cum": ab_cum,
                     "rows": rows, "mixc": mixc, "lev0t": lev0t, "level": level, "uw": uw, "state": state, "o": o,
                     "onorm": onorm, "mix": mix, "res1": res1, "res2": res2, "sum2": sum2,
                     "res3": res3, "sqh": sqh, "rmsh": rmsh,
                     "att_s": att_s_, "att_t": att_t, "att_o": att_o, "ret_o": ret_o, "ret_t": ret_t, "ret_x": ret_x,
                     "mix2": mix2, "ffn2": ffn2}
            for n in range(-1, NB):
                if n == -1:
                    x0()
                    for m in range(1, 3):
                        split(m)
                        if m == 1:
                            act.wait_ge(sem["abw"], 16)
                            act.activation(abh[:], abw, ACT.Copy).then_inc(sem["abh"], 1)
                            act.activation(onesr[:], ones, ACT.Copy).then_inc(sem["onr"], 1)
                    continue
                if n + 3 < NB and n not in URGENT:
                    split(n + 3)
                for step, a in TODO[n]:
                    if step in steps:
                        steps[step](*a)
                if n + 3 < NB and n in URGENT:
                    split(n + 3)

        @block.vector
        def _(dve):
            def tt(out, a, b, op, name):
                dve.tensor_tensor(out, a, b, op).then_inc(sem[name], 1)

            def stt(out, a, s, b, op0, op1, name):
                dve.scalar_tensor_tensor(out=out, in0=a, scalar=s, in1=b, op0=op0, op1=op1).then_inc(sem[name], 1)

            def split(n):
                if n in POOL_LOW:
                    return
                dve.wait_ge(sem["wh"], n + 1)
                if n - 1 in POOL_LOW:
                    dve.wait_ge(sem["wl"], n)
                tt(wl[:, n % 3], raw[:, n % 2], f32(wh[:, n % 3]), ALU.subtract, "wl")

            def low(dst, src, hi, name_hi, v, name):
                dve.wait_ge(sem[name_hi], v)
                tt(dst, src, f32(hi), ALU.subtract, name)

            def take(n):
                key = kind, j = SEQ[n]
                if key not in RING:
                    return
                dve.wait_ge(sem["mm"], n + 1)
                ps = ring(key)[:]
                if kind in YKINDS:
                    if key == ("k", 0):
                        dve.wait_ge(sem["rb"], 1)
                    if kind == "u1" and j == 0:
                        dve.wait_ge(sem["rb"], 2)
                    before = SEQ[n - 2] if n >= 2 else None
                    if before in TAPS:
                        dve.wait_ge(sem["cv"], TAPS[before])
                    if before in SIG:
                        dve.wait_ge(sem["sg"], SIG[before] + 1)
                    if before and before[0] in ("z", "gr"):
                        dve.wait_ge(sem["zs" if before[0] == "z" else "sr"], before[1] + 1)
                    tt(y[n % 2][:], ps, two(rb[:]), ALU.mult, "ev")
                elif kind == "c":
                    if j:
                        dve.wait_ge(sem["cx"], j)
                    tt(cg[:], ps, two(rb[:]), ALU.mult, "ev")
                elif kind == "b":
                    if j:
                        dve.wait_ge(sem["mc"], j)
                    tt(bg[:], ps, two(rb[:]), ALU.mult, "ev")
                elif kind == "wa":
                    dve.wait_ge(sem["sg"], SIG[("ga", j)] + 1)
                    tt(pair(m1, j), ps, e[j % 2][:], ALU.mult, "ev")
                elif kind == "wb":
                    dve.wait_ge(sem["sg"], SIG[("gb", j)] + 1)
                    tt(t2[j % 2][:], ps, pair(sgb, j), ALU.mult, "ev")
                elif kind in ("qa", "ka", "qr", "kr"):
                    if kind == "qa" and j == 0:
                        dve.wait_ge(sem["rb"], 3)
                    tt(pair({"qa": qa, "ka": ka, "qr": qr, "kr": kr}[kind], j), ps, two(rb[:]), ALU.mult, "ev")
                elif kind in ("va", "vr"):
                    if kind == "va" and j == 0:
                        dve.wait_ge(sem["rtk"], 1)
                    if kind == "vr" and j == 0:
                        dve.wait_ge(sem["as"], 8)
                    tt((va if kind == "va" else vr)[:, :, j * S:(j + 1) * S], ps,
                       rtok[:].unsqueeze(2).broadcast_to([P, 2, S]), ALU.mult, "ev")
                elif kind == "pb":
                    dve.wait_ge(sem["sg"], SIG[("tb", j // 2)] + 1)
                    if j < 4:
                        dve.wait_ge(sem["or"], 8)
                    tt(t2[j // 2 % 2][:], ps, tb(j // 2), ALU.mult, "ev")
                elif kind == "u2":
                    if j == 0:
                        dve.wait_ge(sem["rb"], 4)
                    if j >= 2:
                        dve.wait_ge(sem["fq2"], j - 1)
                    stt(y[j % 2][:], ps, 0.0, two(rb[:]), ALU.max, ALU.mult, "ev")

            def x0():
                dve.memset(G2[:], 0.0).then_inc(sem["g2z"], 1)
                dve.wait_ge(sem["par"], 16)
                tt(gg, par[:, PAR["g_fin"]:PAR["g_fin"] + 8], par[:, PAR["g_n1"]:PAR["g_n1"] + 8], ALU.mult, "gg")
                for half, (w_there, done) in enumerate((("wh0", "wl0"), ("wh", "wl"))):
                    for k in range(4 * half, 4 * half + 4):
                        dve.wait_ge(sem["x0h"], k + 1)
                        stt(Xl[:, k], xT[:, k], pcol("g_mix", k), f32(Xh[:, k]), ALU.mult, ALU.subtract, "x0")
                    dve.wait_ge(sem[w_there], 1)
                    pairs_ = slice(8 * half, 8 * half + 8)
                    tt(wl[:, 0, pairs_], raw[:, 0, pairs_], f32(wh[:, 0, pairs_]), ALU.subtract, done)

            def norm(i):
                dve.wait_ge(sem["nl"], 4)
                tt(lnt[:], psA[5][:, 1], rfin[:], ALU.mult, "ms0")
                dve.wait_ge(sem["ms0"], 1)
                tt(lnt[:], lnt[:], rfin[:], ALU.mult, "ms")
                dve.wait_ge(sem["nl"], 6)
                tt(rb[:], lnt[:], rfin[:], ALU.mult, "rb")

            def conv(a, cols, taps):
                i = CONV[a]
                dve.wait_ge(sem["tap"], i + 1)
                first = TAPS[a] - 2 * (taps - 1)
                for d in range(1, taps):
                    for f in range(2):
                        if d > 1:
                            dve.wait_ge(sem["cv"], first + 2 * (d - 2) + f + 1)
                        stt(acc[i % 2][:, f, d:S], yk(a)[:, f, 0:S - d], cols(taps - 1 - d, f), acc[i % 2][:, f, d:S],
                            ALU.mult, ALU.add, "cv")

            def conv4(kind, j):
                c = {"q": 0, "k": 8, "v": 16}[kind] + 2 * j
                conv((kind, j), lambda tap, f: pcol("conv_g", 24 * tap + c + f), 4)

            def gatec(j):
                conv(("x", j), lambda tap, f: pcol("conv_a", 8 * tap + 2 * j + f), 3)

            def conv3(j):
                conv(("u1", j), lambda tap, f: pcol("conv_f", 2 * FF1 * tap + j + f * FF1), 3)

            def zg(j):
                low(pair(Yl, j), t2[j % 2][:], pair(Yh, j), "ogh", j + 1, "og")

            def ffn1(j):
                h, l = ((Xh, Xl), (Zh, Zl), (Xh, Xl))[j // 8]
                low(l[:, j % 8], t2[j % 2][:, 1], h[:, j % 8], "f1h", j + 1, "f1")

            def then(n, ins):
                ins.then_inc(sem["abv"], 1)
                dve.wait_ge(sem["abv"], n)

            def ab_mm():
                dve.wait_ge(sem["ab"], 1)
                dve.wait_ge(sem["g2z"], 1)
                then(1, dve.tensor_tensor(abt[:, 0], psA[4][0:64, 0], rb[0:64], ALU.mult))
                u, m = abt[0:8, 1], abt[0:8, 2]
                then(2, dve.tensor_scalar(u, abt[0:8, 0], pcol("dt_b", hi=8), None, ALU.add))
                then(3, dve.scalar_tensor_tensor(out=m, in0=u, scalar=-1.0, in1=u, op0=ALU.mult, op1=ALU.max))

            def ab_gates():
                dve.wait_ge(sem["aba"], 3)
                then(4, dve.tensor_scalar(den, abt[:, 0], 1.0, None, ALU.add))
                then(5, dve.scalar_tensor_tensor(out=G2[0:8], in0=den[0:8], scalar=-1.0, in1=abt[0:8, 0], op0=ALU.add,
                                                 op1=ALU.subtract))
                dve.wait_ge(sem["aba"], 4)
                then(6, dve.reciprocal(den, den))
                dve.tensor_copy(G2[32:40], den[32:40]).then_inc(sem["g2"], 1)

            def ab_decay():
                u, m, g = abt[0:8, 1], abt[0:8, 2], G2[0:8]
                then(7, dve.tensor_tensor(g, g, den[0:8], ALU.mult))
                then(8, dve.tensor_tensor(g, m, g, ALU.subtract))
                then(9, dve.scalar_tensor_tensor(out=g, in0=u, scalar=0.0, in1=g, op0=ALU.max, op1=ALU.add))
                dve.tensor_scalar(g, g, small[0:8, 8:9], -1.0, ALU.mult, ALU.mult).then_inc(sem["g2"], 1)

            def ab_tok():
                dve.wait_ge(sem["abT"], 1)
                dve.tensor_copy(gtok[:], flat(4)[:, 0:80].rearrange("p (t c) -> p t c", t=2)).then_inc(sem["gtok"], 1)

            def ab_cum():
                dve.wait_ge(sem["cum"], 1)
                dve.tensor_copy(Gs[:], flat(4)[:, 0:64]).then_inc(sem["gs"], 1)
                dve.tensor_copy(G3, psA[4][0:8, 1]).then_inc(sem["g3"], 1)
                dve.wait_ge(sem["gs"], 1)
                ht = "p (t h) -> p h t"
                dve.tensor_scalar(TS[:, 0], Gs[:, 0:16].rearrange(ht, t=2), -1.0, None, ALU.mult).then_inc(sem["gs"], 1)
                tt(TS[:, 3], Gs[:, 16:32].rearrange(ht, t=2), Gs[:, 0:16].rearrange(ht, t=2), ALU.subtract, "gs")
                dve.tensor_copy(TS[:, 1], gtok[:, :, 32:40].rearrange("p t h -> p h t")).then_inc(sem["tb"], 1)
                dve.wait_ge(sem["tb"], 1)
                dve.wait_ge(sem["tsa"], 1)
                tt(TS[:, 2], TS[:, 1], TS[:, 4], ALU.mult, "tb")

            def rows(h):
                dve.wait_ge(sem["row"], h + 1)
                dve.wait_ge(sem["kn"], 8)
                tt(kb[:, h], kn[:, h], psA[4 * (h % 2)][:, 0], ALU.mult, "kb")
                tt(DT[:, h].rearrange("p (t m) -> p t m", t=2), psA[4 * (h % 2) + 1][:, 1].rearrange("p (t m) -> p t m", t=2),
                   negm.unsqueeze(1).broadcast_to([P, 2, P]), ALU.add, "kb")

            def kk(h):
                dve.wait_ge(sem["kk"], h + 1)
                dve.wait_ge(sem["dt"], h + 1)
                v = psA[2 + h % 2][:].rearrange("p t (w m) -> p t w m", w=2)
                d = DT[:, h].rearrange("p (t m) -> p t m", t=2)
                tt(LT[:, h].rearrange("p (t m) -> p t m", t=2), v[:, :, 0], d, ALU.mult, "lt")
                tt(AQ[:, h].rearrange("p (t m) -> p t m", t=2), v[:, :, 1], d, ALU.mult, "lt")

            def tok(b):
                def col(i):
                    return TS[:, i, 2 * b:2 * b + 2].unsqueeze(3).broadcast_to([P, 2, 2, P])

                dve.wait_ge(sem["tk"], 2 * b + 1)
                if b == 0:
                    dve.wait_ge(sem["tb"], 2)
                    dve.wait_ge(sem["tsa"], 3)
                v = psA[4][:].rearrange("p a (c m) -> p a c m", m=P)
                tt(KBE[:, 2 * b:2 * b + 2], v, col(2), ALU.mult, "tok")
                tt(KD[:, 2 * b:2 * b + 2], v, col(3), ALU.mult, "tok")
                dve.wait_ge(sem["tk"], 2 * b + 2)
                v = psA[5][:].rearrange("p a (c m) -> p a c m", m=P)
                tt(VB[:, 2 * b:2 * b + 2], v, col(1), ALU.mult, "tok")

            def level(l):
                for b in range(4):
                    i = 4 * l + b
                    dve.wait_ge(sem["pb_"], i + 1)
                    for q, dst in enumerate((SI, TI)[:2 if l < 4 else 1]):
                        v = dst[:, 2 * b:2 * b + 2]
                        tt(v, v, psA[2 * (b % 2) + q][:].rearrange("p a (c m) -> p a c m", m=P), ALU.subtract, "st")

            def state(c):
                if c:
                    dve.wait_ge(sem["sp"], c + 1)
                    dve.wait_ge(sem["dec"], c)
                    for q in range(2):
                        tt(hist[c][:, 4 * q:4 * q + 4], dec[:, 4 * q:4 * q + 4], quad(4 + q), ALU.add, "h")

            def wstate(c):
                t, r = c // 2, slice(CHUNK * (c % 2), CHUNK * (c % 2) + CHUNK)
                dve.wait_ge(sem["ws"], c)
                for q in range(2):
                    v = U[r, 4 * q:4 * q + 4, t]
                    tt(v, v, psA[q][r].rearrange("p a (c m) -> p (a c) m", m=P), ALU.subtract, "vn")

            def onorm(q):
                dve.wait_ge(sem["ri"], HEADN[(q,)] + 1)
                v = pair(OT, q)
                stt(v, v, pcol("g_o"), t2[q % 2][:], ALU.mult, ALU.mult, "on")

            def mixc(j):
                low(pair(Yl, j), t2[j % 2][:], pair(Yh, j), "yah", j + 1, "ya")

            def mix(j):
                low(pair(Xl, j), t2[j % 2][:], pair(Xh, j), "mxh", j + 1, "mx")

            def gained(dst, hi, gain, name_hi, name, j):
                for k in (2 * j, 2 * j + 1):
                    dve.wait_ge(sem[name_hi], k + 1)
                    stt(dst[:, k], xT[:, k], gain(k), f32(hi[:, k]), ALU.mult, ALU.subtract, name)

            def complete(kind, j):
                if j % 2:
                    dve.wait_ge(sem["mm"], AT[(kind, 2 + j // 2)] + 1)
                else:
                    dve.wait_ge(sem["half"], HALF[(kind, 2 + j // 2)])

            def res1(j):
                complete("wo", j)
                if j == 0:
                    dve.wait_ge(sem["xres"], 16)
                    dve.wait_ge(sem["mx0"], 4)
                tt(pair(xT, j), psA[j][:], pair(xres, j), ALU.add, "r1")
                gained(Yl, Yh, lambda k: pcol("g_ffn", k), "x1h", "x1", j)

            def res2(j):
                if j == 2:
                    dve.wait_ge(sem["half"], HALF[("d1", 10)])
                else:
                    dve.wait_ge(sem["mm"], AT[("d1", (8, 9, 10, 10)[j])] + 1)
                tt(pair(xT, j), psA[j][:], pair(xT, j), ALU.add, "r2")
                gained(Yl, Yh, lambda k: gg[:, k:k + 1], "xbh", "xb", j)

            def res3(j):
                complete("w2", j)
                tt(pair(xT, j), psA[j][:], pair(xT, j), ALU.add, "r3")
                gained(Xl, Xh, lambda k: pcol("g_n2", k), "x3h", "x3", j)

            def x2():
                for k in range(KT):
                    stt(xT[:, k], xT[:, k], pcol("g_fin", k), rfin[:], ALU.mult, ALU.mult, "x2")

            def rtok_():
                dve.wait_ge(sem["rtp"], 1)
                dve.tensor_copy(rtok[:], flat(4)[:, 0:2]).then_inc(sem["rtk"], 1)

            def rmsh(kind, j):
                i = HEADN[(kind, j)]
                dve.wait_ge(sem["ri"], i + 1)
                for f in range(2):
                    v = QK[kind][:, 2 * j + f]
                    stt(v, v, pcol("g_q" if kind == "qa" else "g_k", 2 * j + f), t2[i % 2][:, f], ALU.mult, ALU.mult, "qk")

            def att_s_(i):
                hp, t = i // 2, i % 2
                n = P * (t + 1)
                dve.wait_ge(sem["as"], i + 1)
                if i == 0:
                    dve.wait_ge(sem["md"], 16)
                if i >= 2:
                    dve.wait_ge(sem["at"], i - 1)
                buf = att_s[i % 2].rearrange("p a b -> p (a b)")
                for g in range(3):
                    slope = float(np.float32(2.0 ** (-8.0 * (4 * g + hp + 1) / HA)))
                    src = flat(0)[:, g * P:(g + 1) * P] if t == 0 else psA[2 + g // 2][:, g % 2]
                    stt(buf[:, g * n:(g + 1) * n], md[:, g, S - n:S], -slope / SCALE, src, ALU.mult, ALU.add, "sc")
                dve.wait_ge(sem["sc"], 3 * i + 3)
                dve.tensor_reduce(atn[:, t, 0:1], buf[:, 0:3 * n], AX.X, ALU.max).then_inc(sem["am"], 1)
                dve.wait_ge(sem["am"], i + 1)
                dve.tensor_scalar(atn[:, t, 1:2], atn[:, t, 0:1], -SCALE, None, ALU.mult).then_inc(sem["nm"], 1)
                dve.wait_ge(sem["pe"], i + 1)
                dve.reciprocal(atn[:, t, 3:4], atn[:, t, 2:3]).then_inc(sem["rd"], 1)
                dve.wait_ge(sem["rd"], i + 1)
                dve.tensor_scalar(buf[:, 0:3 * n], buf[:, 0:3 * n], atn[:, t, 3:4], None, ALU.mult).then_inc(sem["pn"], 1)

            def att_o(i):
                s = slice(i % 2 * P, (i % 2 + 1) * P)
                low(Ol[:, i // 2, s], quad(1)[:, 0], Oh[:, i // 2, s], "oah", i + 1, "oa")

            def ret_s(h):
                dve.wait_ge(sem["rsp"], h + 1)
                if h == 0:
                    dve.wait_ge(sem["dr"], 16)
                b = 2 * (h % 2)
                tt(ST[h][:, 0:S], psA[b][:, 0], dr[:, h], ALU.mult, "rs")
                tt(ST[h][:, S:S + P], psA[b][:, 1, 0:P], dr[:, h, 0:P], ALU.mult, "rs")

            def ret_o(i):
                dve.wait_ge(sem["ro"], i + 1)
                dve.bn_stats(bst[:, i % 2], flat(4 + i % 2)).then_inc(sem["bst"], 1)
                dve.wait_ge(sem["bst"], i + 1)
                dve.bn_aggr(bag[:, i % 2], bst[:, i % 2]).then_inc(sem["bag"], 1)
                dve.wait_ge(sem["rr"], i + 1)
                if i >= 2:
                    dve.wait_ge(sem["rtT"], i - 1)
                dve.tensor_scalar(acc[i % 2][:], psA[4 + i % 2][:], bag[:, i % 2, 0:1], rsd[:, i % 2, 1:2],
                                  ALU.subtract, ALU.mult).then_inc(sem["ry"], 1)

            def ret_x(i):
                h, t = i // 2, i % 2
                s = (slice(None), slice(4 * (h % 2), 4 * (h % 2) + 4), slice(t * P, (t + 1) * P))
                low((Zl, Xl)[h // 2][s], t2[i % 2][:].rearrange("p a (c m) -> p (a c) m", m=P), (Zh, Xh)[h // 2][s],
                    "orh", i + 1, "or")

            def ma():
                dve.wait_ge(sem["mm"], AT[("pa", 1)] + 1)
                dve.wait_ge(sem["sg"], SIG[("ta", 3)] + 1)
                for q in range(4):
                    tt(pair(ta, q), psA[q][:], pair(ta, q), ALU.mult, "ma")

            def mix2(j):
                low(pair(Yl, j), t2[j % 2][:], pair(Yh, j), "m2h", j + 1, "m2")

            def ffn2(j):
                dve.wait_ge(sem["fq2"], j + 1)
                h, l = ((Yh, Yl), (Zh, Zl))[j // 4 % 2]
                low(pair(l, j % 4), t2[j % 2][:], pair(h, j % 4), "f2h", j + 1, "f2")

            def res4(q):
                dve.wait_ge(sem["mm"], AT[("d2", 12 + q)] + 1)
                tt(pair(xT, q), psA[q][:], pair(xT, q), ALU.add, "res4")

            steps = {"gatec": gatec, "conv3": conv3,
                     "zg": zg, "ffn1": ffn1, "ab_mm": ab_mm, "ab_gates": ab_gates, "ab_decay": ab_decay, "ab_tok": ab_tok, "ab_cum": ab_cum,
                     "rows": rows, "kk": kk, "tok": tok, "level": level, "state": state, "wstate": wstate,
                     "onorm": onorm, "mixc": mixc, "mix": mix, "res1": res1, "res2": res2, "res3": res3, "x2": x2,
                     "rtok": rtok_, "rmsh": rmsh, "att_s": att_s_, "att_o": att_o, "ret_s": ret_s, "ret_o": ret_o,
                     "ret_x": ret_x, "ma": ma, "mix2": mix2, "ffn2": ffn2, "res4": res4}
            for n in range(-1, NB):
                if n == -1:
                    x0()
                    for m in range(1, 3):
                        split(m)
                        if m == 1:
                            dve.wait_ge(sem["abh"], 1)
                            tt(abl[:], abw, f32(abh[:]), ALU.subtract, "abl")
                    continue
                if ("norm", (2,)) in TODO[n]:
                    norm(2)
                take(n)
                for step, a in TODO[n]:
                    if step == "conv4":
                        conv4(*a)
                if n + 3 < NB and n not in URGENT:
                    split(n + 3)
                for step, a in TODO[n]:
                    if step in steps:
                        steps[step](*a)
                if n + 3 < NB and n in URGENT:
                    split(n + 3)

        @block.gpsimd
        def _(pool):
            def tt(out, a, b, op, name):
                pool.tensor_tensor(out, a, b, op).then_inc(sem[name], 1)

            def x0():
                for j in range(4):
                    if j % 2 == 0:
                        pool.wait_ge(sem["xTb" if j else "xT"], 16)
                    if j >= 2:
                        pool.wait_ge(sem["ss0"], j - 1)
                    tt(sq[j % 2][:] if j else ss[0][:], pair(xT, j), pair(xT, j), ALU.mult, "sq0")
                    pool.wait_ge(sem["sq0"], j + 1)
                    if j:
                        if j > 1:
                            pool.wait_ge(sem["ss0"], j - 1)
                        tt(ss[0][:], ss[0][:], sq[j % 2][:], ALU.add, "ss0" if j < 3 else "ss")

            def silu(kind, j):
                if kind != "v":
                    m = HEADN[(kind, j)]
                    pool.wait_ge(sem["silu"], SILU[(kind, j)] + 1)
                    if m >= 2:
                        pool.wait_ge(sem["hsum"], m - 1)
                    else:
                        pool.wait_ge(sem["ss"], 1)
                    dst = pair(QKV[kind], j)
                    tt(sq[m % 2][:], dst, dst, ALU.mult, "sq")

            def l2n(kind, j):
                pool.wait_ge(sem["ri"], HEADN[(kind, j)] + 1)
                v = pair(QKV[kind], j)
                tt(v, v, t2[HEADN[(kind, j)] % 2][:], ALU.mult, "kn")

            def gatec(j):
                pool.wait_ge(sem["ev"], GRP[("x", j)] + 1)
                v = y[AT[("x", j)] % 2][:]
                tt(v, v, cg[:], ALU.mult, "cx")

            def mixc(j):
                pool.wait_ge(sem["cv"], TAPS[("x", j)])
                pool.wait_ge(sem["ev"], GRP[("b", j)] + 1)
                pool.wait_ge(sem["ya"], j - 1) if j >= 2 else pool.wait_ge(sem["qd"], 8)
                tt(t2[j % 2][:], acc[CONV[("x", j)] % 2][:], bg[:], ALU.mult, "mc")

            def rows(h):
                pool.wait_ge(sem["eg"], h + 1)
                if h == 0:
                    pool.wait_ge(sem["kn"], 8)
                tt(qd[:, h], qn[:, h], t2[h % 2][:, 0], ALU.mult, "qd")

            def lev0():
                pool.wait_ge(sem["mask"], 16)
                pool.wait_ge(sem["kk"], 8)
                for b in range(4):
                    pool.wait_ge(sem["lt"], 4 * b + 4)
                    if b >= 2:
                        pool.wait_ge(sem["s0"], 2 * b - 2)
                    v = LT[:, 2 * b:2 * b + 2].rearrange("p h (t m) -> p (h t) m", m=P)
                    s = sq[b % 2][:].rearrange("p a (c m) -> p (a c) m", m=P)
                    tt(s, v, mask[:, 0].unsqueeze(1).broadcast_to([P, 4, P]), ALU.mult, "s0")
                    pool.wait_ge(sem["s0"], 2 * b + 1)
                    tt(SI[:, 2 * b:2 * b + 2].rearrange("p h t m -> p (h t) m"),
                       ident.unsqueeze(1).broadcast_to([P, 4, P]), s, ALU.subtract, "s0")

            def level(l):
                for b in range(4):
                    i = 4 * l + b
                    if i >= 2:
                        pool.wait_ge(sem["pa_"], i - 1)
                    else:
                        pool.wait_ge(sem["s0"], 8)
                    v = LT[:, 2 * b:2 * b + 2].rearrange("p h (t m) -> p (h t) m", m=P)
                    tt(sq[b % 2][:].rearrange("p a (c m) -> p (a c) m", m=P), v,
                       mask[:, l + 1].unsqueeze(1).broadcast_to([P, 4, P]), ALU.mult, "bs")

            def state(c):
                if c == 2:
                    return
                pool.wait_ge(sem["h0"], 2) if c == 0 else pool.wait_ge(sem["h"], 2)
                tt(dec, hist[c], egl[:, c + 1].unsqueeze(2).broadcast_to([P, H1, P]), ALU.mult, "dec")

            def osq(q):
                m = HEADN[(q,)]
                pool.wait_ge(sem["oc"], 4)
                pool.wait_ge(sem["hsum"], m - 1)
                if q < 2:
                    pool.wait_ge(sem["pa_"], 20)
                tt(sq[m % 2][:], pair(OT, q), pair(OT, q), ALU.mult, "sq")

            def sqh(kind, j):
                i = HEADN[(kind, j)]
                pool.wait_ge(sem["ev"], GRP[(kind, j)] + 1)
                if i == 12:
                    pool.wait_ge(sem["ss"], 3)
                tt(sq[i % 2][:], pair(QK[kind], j), pair(QK[kind], j), ALU.mult, "sqp")
                pool.wait_ge(sem["sqp"], i - 11)
                pool.wait_ge(sem["sqh"], i - 11)
                pool.wait_ge(sem["hsum"], i - 1)
                tt(pair(Zl, i % 2), sq[i % 2][:], f32(pair(Zh, i % 2)), ALU.subtract, "sq")

            def zg(j):
                pool.wait_ge(sem["zs"], j + 1)
                pool.wait_ge(sem["on"], 4)
                if j >= 2:
                    pool.wait_ge(sem["og"], j - 1)
                tt(t2[j % 2][:], e[j % 2][:], pair(OT, j), ALU.mult, "zp")

            def mix(j):
                pool.wait_ge(sem["ev"], GRP[("wb", j)] + 1)
                tt(t2[j % 2][:], t2[j % 2][:], pair(m1, j), ALU.add, "mx0")

            def add_squares(i, j):
                base = {1: 0, 2: 2, 3: 7}[i]
                per = 2 if i == 2 else 1
                done = {1: 0, 2: 4, 3: 12}[i]
                if j == 0:
                    return
                for g in range(per):
                    pool.wait_ge(sem["sqr"], done + per * j + g + 1)
                    src = (sq, t2)[g][j % 2][:]
                    last = j == 3 and g == per - 1
                    name = "ss" if last else "ssa"
                    if j > 1:
                        pool.wait_ge(sem["ssa"], base + per * (j - 2) + g + 1)
                    tt(ss[g][:], ss[g][:], src, ALU.add, name)

            def ffn1(j):
                pool.wait_ge(sem["fs"], j + 1)
                pool.wait_ge(sem["f1"], j - 1) if j >= 2 else pool.wait_ge(sem["mx"], 4)
                tt(t2[j % 2][:, 1], e[j % 2][:, 0], acc[CONV[("u1", j)] % 2][:, 1], ALU.mult, "fp")

            def ret_t(i):
                h, t = i // 2, i % 2
                pool.wait_ge(sem["rt"], i + 1)
                pool.wait_ge(sem["sr"], 2 * h + 2)
                v = t2[i % 2][:].rearrange("p a (c m) -> p (a c) m", m=P)
                tt(v, v, gr[:, 4 * h:4 * h + 4, t * P:(t + 1) * P], ALU.mult, "rg")

            def mix2(j):
                pool.wait_ge(sem["ev"], GRP[("pb", 2 * j)] + 1)
                pool.wait_ge(sem["ma"], 4)
                tt(t2[j % 2][:], t2[j % 2][:], pair(ta, j), ALU.add, "m20")

            def ffn2(j):
                pool.wait_ge(sem["ev"], GRP[("u2", j)] + 1)
                pool.wait_ge(sem["f2"], j - 1) if j >= 2 else pool.wait_ge(sem["m2"], 4)
                tt(t2[j % 2][:], y[j % 2][:], y[j % 2][:], ALU.mult, "fq2")

            steps = {"x0": x0, "silu": silu, "l2n": l2n, "gatec": gatec, "mixc": mixc, "rows": rows,
                     "lev0": lev0, "level": level, "state": state, "osq": osq, "sqh": sqh, "zg": zg, "mix": mix,
                     "res1": lambda j: add_squares(1, j), "sum2": lambda j: add_squares(2, j),
                     "res3": lambda j: add_squares(3, j), "ffn1": ffn1, "ret_t": ret_t,
                     "mix2": mix2, "ffn2": ffn2}
            for n in range(-1, NB):
                if n + 3 in POOL_LOW:
                    pool.wait_ge(sem["wl"], n + 3)
                    pool.wait_ge(sem["wh"], n + 4)
                    tt(wl[:, n % 3], raw[:, (n + 3) % 2], f32(wh[:, n % 3]), ALU.subtract, "wl")
                for step, a in TODO[n]:
                    if step in steps:
                        steps[step](*a)


def blocks(matrix, name):
    w = matrix.reshape(matrix.shape[0] // P, P, matrix.shape[1] // P, P)
    at = [(n, pairs(*key)[1]) for n, key in enumerate(SEQ) if pairs(*key)[0] == name]
    k = np.array([[a for a, _ in prs] for _, prs in at])
    c = np.array([[b for _, b in prs] for _, prs in at])
    return [n for n, _ in at], w[k, :, c, :].transpose(0, 2, 1, 3)


def channels(a):
    return a.reshape(-1, P).T


def delta_constants():
    j, i = np.arange(P)[:, None], np.arange(P)[None, :]
    same = j // CHUNK == i // CHUNK
    sums = [np.where(same & (i >= j), 0.0, NEG)]
    cols = []
    for s in (1, 2, 4, 8, 16, 32):
        cols.append((j // (2 * s) == i // (2 * s)) & (i % (2 * s) >= s) & (j % (2 * s) < s))
    sums += [same & (j <= i), same, (j < CHUNK) & (i >= 0), (j >= CHUNK) & (i >= 0)]
    return [np.stack([c.astype(np.float32) for c in v], axis=1) for v in (sums, cols)]


def attention_constants():
    i, j = np.arange(P)[:, None] + P, np.arange(S)[None, :]
    d = i - j
    return np.concatenate([np.where((d >= 0) & (d % dil == 0) & (d <= reach), d, BIG).astype(np.float32)
                           for dil, reach in ((1, 128), (4, 512), (16, 2048))], axis=1)


def retention_constants():
    j, i = np.arange(P)[:, None], np.arange(S)[None, :]
    cols = []
    for h in range(RH):
        log_g = np.log(1.0 - 2.0 ** (-5.0 - h))
        cols.append(np.where(i >= j, np.exp(log_g * np.maximum(i - j, 0)) * 256.0 ** -0.5, 0.0).astype(np.float32))
    return np.concatenate(cols, axis=1)


def kernel(**inputs):
    import concourse.bacc as bacc
    from concourse.bass_utils import run_bass_kernel_spmd

    a = {name: np.asarray(v) for name, v in inputs.items()}
    w_in = a["w_in"][0]
    wts = np.empty((NB, P, 16, P), np.float32)
    for name, m in (("w_in", w_in[:, :7168]), ("w_gates", w_in[:, 7184:]), ("w_a_out", a["w_a_out"][0]),
                    ("w_b_out", a["w_b_out"][0]), ("w_o", a["w_o"][0]), ("w_up", a["w_up"][0]),
                    ("w_down", a["w_down"][0]), ("w_in_2", a["w_in_2"][0]), ("w_proj_a_2", a["w_proj_a_2"][0]),
                    ("w_proj_b_2", a["w_proj_b_2"][0]), ("w_out_2", a["w_out_2"][0]), ("w_up_2", a["w_up_2"][0]),
                    ("w_down_2", a["w_down_2"][0])):
        at, b = blocks(m, name)
        wts[at] = b
    par = np.zeros((P, NPAR), np.float32)
    for name, v in (("g_mix", "norm_mix_g"), ("conv_a", "conv_a_w"), ("conv_g", "gdn_conv_w"), ("g_ffn", "norm_ffn_g"),
                    ("conv_f", "ffn_conv_w"), ("g_fin", "norm_final_g"), ("g_n1", "norm1_g_2"), ("g_q", "q_norm_g_2"),
                    ("g_k", "k_norm_g_2"), ("gn_g", "ret_gn_g_2"), ("gn_b", "ret_gn_b_2"), ("g_n2", "norm2_g_2"),
                    ("g_o", "gdn_norm_g")):
        v = channels(a[v])
        par[:, PAR[name]:PAR[name] + v.shape[1]] = v
    par[0:8, PAR["a_log"]] = a["gdn_A_log"][0]
    par[0:8, PAR["dt_b"]] = a["gdn_dt_bias"][0]
    par[:, PAR["eps"]] = EPS
    par[:, PAR["one"]] = 1.0
    par[:, PAR["ln_scale"]] = np.log(SCALE)
    par[:, PAR["ident"]:PAR["ident"] + P] = np.eye(P)
    par[:, PAR["ones"]:PAR["ones"] + P] = 1.0
    abw = np.zeros((P, KT, 64), np.float32)
    ab = w_in[:, 7168:7184].reshape(KT, P, 16).transpose(1, 0, 2)
    abw[:, :, 0:8], abw[:, :, 32:40] = ab[:, :, 0:8], ab[:, :, 8:16]
    sel = np.zeros((P, H1, P), np.float32)
    for h in range(H1):
        sel[h, h], sel[32 + h, h] = 1.0, 1.0
    sums, masks = delta_constants()
    x = a["x"][0].reshape(S, KT, P).transpose(2, 1, 0)
    arrays = {"wts": wts, "par": par, "x": x, "abw": abw, "sums": sums, "mask": masks, "sel": sel,
              "md": attention_constants(), "dr": retention_constants()}
    nc = bacc.Bacc("TRN2", target_bir_lowering=False, num_devices=1)
    args = []
    for name, v in arrays.items():
        arrays[name] = np.ascontiguousarray(v)
        args.append(nc.dram_tensor("in_" + name, v.shape, F32, kind="ExternalInput").ap())
    args.append(nc.dram_tensor("out", (P, KT, S), F32, kind="ExternalOutput").ap())
    program(nc, *args)
    r = run_bass_kernel_spmd(nc, [{"in_" + name: v for name, v in arrays.items()}], core_ids=[0])
    out = r.results[0]["out"]
    return out.transpose(2, 1, 0).reshape(1, S, D)
```
